# Optimizing a Trainium2 kernel written in Bass

```python
import jax, jax.numpy as jnp
from jax import lax
import numpy as np

D_MODEL = 1024
BATCH = 1
SEQ = 512
DEPTH = 1

CHUNK = 64
HEAD_DIM = 64
MIX_W = D_MODEL
FOX_HEADS = (MIX_W // 2) // HEAD_DIM
SWA_HEADS = (MIX_W // 2) // HEAD_DIM
SWA_KV_HEADS = 2
FOX_W = FOX_HEADS * HEAD_DIM
SWA_W = SWA_HEADS * HEAD_DIM
SWA_KV_W = SWA_KV_HEADS * HEAD_DIM
WINDOW = 128
WIN_CHUNKS = WINDOW // CHUNK
Q_BLOCK = 128
PEER_HEADS = 8
PEER_KEYS = 128
PEER_EXPERTS = PEER_KEYS * PEER_KEYS
PEER_QDIM = 256
PEER_TOPK = 16
PEER_TOK_BLOCK = 128
LN_EPS = 1e-5
DN_ALPHA = (2 * DEPTH) ** 0.25
DN_BETA = (8 * DEPTH) ** -0.25
IN_SIZES = (FOX_W, FOX_W, FOX_W, FOX_HEADS, SWA_W, SWA_KV_W, SWA_KV_W)
IN_SPLITS = tuple(int(s) for s in np.cumsum(IN_SIZES)[:-1])
IN_W = sum(IN_SIZES)

kernel_name = "hybrid_fox_swa_sink_peer_deepnorm"

def layer_norm(x, g, b):
    x32 = x.astype(jnp.float32)
    mu = jnp.mean(x32, axis=-1, keepdims=True)
    var = jnp.mean(jnp.square(x32 - mu), axis=-1, keepdims=True)
    y = (x32 - mu) * lax.rsqrt(var + LN_EPS) * g.astype(jnp.float32) + b.astype(jnp.float32)
    return y.astype(x.dtype)

def alibi_slopes(n):
    return 2.0 ** (-8.0 * jnp.arange(1, n + 1, dtype=jnp.float32) / n)

def fox_attention(q, k, v, log_f):
    B, S, H, Dh = q.shape
    nb = S // Q_BLOCK
    c = jnp.cumsum(log_f, axis=1).transpose(0, 2, 1)
    kpos = jnp.arange(S)
    qb = q.reshape(B, nb, Q_BLOCK, H, Dh).transpose(1, 0, 2, 3, 4)
    cb = c.reshape(B, H, nb, Q_BLOCK).transpose(2, 0, 1, 3)
    scale = Dh ** -0.5

    def one_block(args):
        qi, ci, i = args
        s = jnp.einsum('bqhd,bkhd->bhqk', qi, k, preferred_element_type=jnp.float32) * scale
        s = s + ci[..., :, None] - c[:, :, None, :]
        qpos = i * Q_BLOCK + jnp.arange(Q_BLOCK)
        s = jnp.where(kpos[None, :] <= qpos[:, None], s, -jnp.inf)
        p = jax.nn.softmax(s, axis=-1)
        return jnp.einsum('bhqk,bkhd->bqhd', p.astype(v.dtype), v)

    out = lax.map(one_block, (qb, cb, jnp.arange(nb)))
    return out.transpose(1, 0, 2, 3, 4).reshape(B, S, H * Dh)

def swa_sink_attention(q, k, v, sink, slopes):
    B, S, H, Dh = q.shape
    KVH = k.shape[2]
    G = H // KVH
    nc = S // CHUNK
    band = WIN_CHUNKS * CHUNK
    qc = q.reshape(B, nc, CHUNK, KVH, G, Dh)

    def banded(t):
        tc = t.reshape(B, nc, CHUNK, KVH, Dh)
        tp = jnp.pad(tc, ((0, 0), (WIN_CHUNKS - 1, 0), (0, 0), (0, 0), (0, 0)))
        return jnp.concatenate([tp[:, j:j + nc] for j in range(WIN_CHUNKS)], axis=2)

    kb = banded(k)
    vb = banded(v)
    s = jnp.einsum('bcqkgd,bcrkd->bckgqr', qc, kb, preferred_element_type=jnp.float32) * Dh ** -0.5
    qi = jnp.arange(CHUNK)[:, None]
    r = jnp.arange(band)[None, :]
    dist = jnp.abs((WIN_CHUNKS - 1) * CHUNK + qi - r).astype(jnp.float32)
    s = s - slopes.reshape(KVH, G, 1, 1) * dist
    key_chunk = jnp.arange(nc)[:, None] - (WIN_CHUNKS - 1) + jnp.arange(band)[None, :] // CHUNK
    valid = key_chunk >= 0
    s = jnp.where(valid[None, :, None, None, None, :], s, -jnp.inf)
    sk = jnp.broadcast_to(sink.astype(jnp.float32).reshape(1, 1, KVH, G, 1, 1), s.shape[:-1] + (1,))
    p = jax.nn.softmax(jnp.concatenate([s, sk], axis=-1), axis=-1)[..., :band]
    out = jnp.einsum('bckgqr,bcrkd->bcqkgd', p.astype(v.dtype), vb)
    return out.reshape(B, S, H * Dh)

def peer_layer(x, w_q, keys1, keys2, u_tab, v_tab):
    B, S, D = x.shape
    T = B * S
    xt = x.reshape(T, D)
    half = PEER_QDIM // 2
    q = (xt @ w_q).reshape(T, PEER_HEADS, 2, half)
    s1 = jnp.einsum('thd,hnd->thn', q[:, :, 0], keys1).astype(jnp.float32)
    s2 = jnp.einsum('thd,hnd->thn', q[:, :, 1], keys2).astype(jnp.float32)
    v1, i1 = lax.top_k(s1, PEER_TOPK)
    v2, i2 = lax.top_k(s2, PEER_TOPK)
    cand = (v1[..., :, None] + v2[..., None, :]).reshape(T, PEER_HEADS, PEER_TOPK * PEER_TOPK)
    cidx = (i1[..., :, None] * PEER_KEYS + i2[..., None, :]).reshape(T, PEER_HEADS, PEER_TOPK * PEER_TOPK)
    sc, pos = lax.top_k(cand, PEER_TOPK)
    eidx = jnp.take_along_axis(cidx, pos, axis=-1)
    gate = jax.nn.softmax(sc, axis=-1).astype(x.dtype)
    nb = T // PEER_TOK_BLOCK

    def one_block(args):
        xb, eb, gb = args
        u = jnp.take(u_tab, eb, axis=0)
        a = jnp.einsum('nhkd,nd->nhk', u, xb)
        w = jax.nn.gelu(a, approximate=False) * gb
        vv = jnp.take(v_tab, eb, axis=0)
        return jnp.einsum('nhk,nhkd->nd', w, vv)

    y = lax.map(one_block, (xt.reshape(nb, PEER_TOK_BLOCK, D),
                            eidx.reshape(nb, PEER_TOK_BLOCK, PEER_HEADS, PEER_TOPK),
                            gate.reshape(nb, PEER_TOK_BLOCK, PEER_HEADS, PEER_TOPK)))
    return y.reshape(B, S, D)

def setup_inputs(seed: int = 0) -> dict:
    key = jax.random.key(seed)
    ks = jax.random.split(key, 16)
    f32 = jnp.float32
    nrm = lambda k, shp: jax.random.normal(k, shp, dtype=f32)
    x = nrm(ks[0], (BATCH, SEQ, D_MODEL))
    col_scale = jnp.concatenate([
        jnp.ones((2 * FOX_W,), f32), jnp.full((FOX_W,), DN_BETA, f32),
        jnp.ones((FOX_HEADS + SWA_W + SWA_KV_W,), f32),
        jnp.full((SWA_KV_W,), DN_BETA, f32)])
    ln1_g = 1.0 + 0.02 * nrm(ks[1], (DEPTH, D_MODEL))
    ln1_b = 0.02 * nrm(ks[2], (DEPTH, D_MODEL))
    w_in = nrm(ks[3], (DEPTH, D_MODEL, IN_W)) * (D_MODEL ** -0.5) * col_scale
    b_f = 3.0 + 0.5 * nrm(ks[4], (DEPTH, FOX_HEADS))
    sink = 0.5 * nrm(ks[5], (DEPTH, SWA_HEADS))
    w_out = nrm(ks[6], (DEPTH, MIX_W, D_MODEL)) * (MIX_W ** -0.5) * DN_BETA
    ln2_g = 1.0 + 0.02 * nrm(ks[7], (DEPTH, D_MODEL))
    ln2_b = 0.02 * nrm(ks[8], (DEPTH, D_MODEL))
    w_pq = nrm(ks[9], (DEPTH, D_MODEL, PEER_HEADS * PEER_QDIM)) * (D_MODEL ** -0.5)
    peer_keys1 = nrm(ks[10], (DEPTH, PEER_HEADS, PEER_KEYS, PEER_QDIM // 2)) * ((PEER_QDIM // 2) ** -0.5)
    peer_keys2 = nrm(ks[11], (DEPTH, PEER_HEADS, PEER_KEYS, PEER_QDIM // 2)) * ((PEER_QDIM // 2) ** -0.5)
    peer_u = nrm(ks[12], (DEPTH, PEER_EXPERTS, D_MODEL)) * (D_MODEL ** -0.5) * DN_BETA
    peer_v = nrm(ks[13], (DEPTH, PEER_EXPERTS, D_MODEL)) * DN_BETA
    return {"x": x, "ln1_g": ln1_g, "ln1_b": ln1_b, "w_in": w_in, "b_f": b_f, "sink": sink,
            "w_out": w_out, "ln2_g": ln2_g, "ln2_b": ln2_b, "w_pq": w_pq,
            "peer_keys1": peer_keys1, "peer_keys2": peer_keys2, "peer_u": peer_u, "peer_v": peer_v}

def reference(x, ln1_g, ln1_b, w_in, b_f, sink, w_out, ln2_g, ln2_b, w_pq,
              peer_keys1, peer_keys2, peer_u, peer_v):
    B, S, _ = x.shape
    slopes = alibi_slopes(SWA_HEADS)
    for l in range(DEPTH):
        z = x @ w_in[l]
        fq, fk, fv, ff, sq, sk, sv = jnp.split(z, IN_SPLITS, axis=-1)
        log_f = jax.nn.log_sigmoid(ff.astype(jnp.float32) + b_f[l].astype(jnp.float32))
        y_fox = fox_attention(fq.reshape(B, S, FOX_HEADS, HEAD_DIM),
                              fk.reshape(B, S, FOX_HEADS, HEAD_DIM),
                              fv.reshape(B, S, FOX_HEADS, HEAD_DIM), log_f)
        y_swa = swa_sink_attention(sq.reshape(B, S, SWA_HEADS, HEAD_DIM),
                                   sk.reshape(B, S, SWA_KV_HEADS, HEAD_DIM),
                                   sv.reshape(B, S, SWA_KV_HEADS, HEAD_DIM), sink[l], slopes)
        mix = jnp.concatenate([y_fox, y_swa], axis=-1) @ w_out[l]
        x = layer_norm(DN_ALPHA * x + mix, ln1_g[l], ln1_b[l])
        y_peer = peer_layer(x, w_pq[l], peer_keys1[l], peer_keys2[l], peer_u[l], peer_v[l])
        x = layer_norm(DN_ALPHA * x + y_peer, ln2_g[l], ln2_b[l])
    return x


_drawn_inputs = setup_inputs


def setup_inputs(seed=0):
    import zlib

    import numpy as np

    out = dict(_drawn_inputs(seed))
    spreads = {}
    factors = {'sink': 8.0, 'ln2_g': 2.863, 'ln2_b': 2.991}
    for name, (base, spread) in spreads.items():
        noise = np.random.default_rng([zlib.crc32(name.encode()), seed]).standard_normal(out[name].shape)
        drawn = base * np.exp(spread * noise) if base else spread * noise
        out[name] = __import__('jax').numpy.asarray(drawn.astype(out[name].dtype))
    for name, factor in factors.items():
        out[name] = (out[name] * factor).astype(out[name].dtype)
    return out
```

```python
from contextlib import ExitStack

import concourse.bass as bass
from concourse import mybir

F32 = mybir.dt.float32
F32R = mybir.dt.float32r
U32 = mybir.dt.uint32
ALU = mybir.AluOpType
ACT = mybir.ActivationFunctionType
AX_X = mybir.AxisListType.X

P = 128
SEQ = 512
D = 1024
KT = D // P
TB = SEQ // P
HEADS = 8
PAIRS = HEADS // 2
HD = 64
SWA_KEYS = 2 * P
LISTS = 16
PH = 8
TOPK = 16
NKEY = 128
ETILES = 128
EPS = 1e-5
ALPHA = 2.0 ** 0.25
NEG_MAX = -3.0e38

RAW_SLOTS = 4
PART_SLOTS = 2
S_LOOP = 2
S_WOUT = S_LOOP + 4 * PAIRS
S_PQ = S_WOUT + KT
S_U = S_PQ + LISTS
S_V = S_U + ETILES
N_TILES = S_V + ETILES

A_PRE = 56
TOK_PER_TILE = 8
CHUNK = 64
A_MID = SEQ // TOK_PER_TILE
A_POST = ETILES - A_PRE - A_MID
CHUNKS = SEQ // CHUNK
ROUTE_STEPS = 1 + 5 + 2 + 5 + 2 + 2 + 6
TILES_PER_CHUNK = CHUNK // TOK_PER_TILE


def build(nc, x_t, x_rows, w1, w_ff, b_f, sinks, ln_par, w_pq, keys_t, u_t, v_tab, consts, out):
    g_dram = nc.dram_tensor("g_scratch", (CHUNKS, P, ETILES, CHUNK), F32, kind="Internal").ap()
    a_dram = nc.dram_tensor("gelu_scratch", (ETILES // 4, P, 4, SEQ), F32, kind="Internal").ap()
    c_dram = nc.dram_tensor("decay_scratch", (4, HEADS, SEQ), F32R, kind="Internal").ap()

    ctx = ExitStack()
    with ctx:
        def sb(name, shape, dt=F32, stack=ctx):
            return stack.enter_context(nc.sbuf_tensor(name, shape, dt))

        def sem(name):
            return ctx.enter_context(nc.semaphore(name))

        raw = sb("raw", [P, RAW_SLOTS, D])
        hi = [sb(f"hi{i}", [P, D], F32R) for i in range(PART_SLOTS)]
        lo = [sb(f"lo{i}", [P, D], F32R) for i in range(PART_SLOTS)]
        x1 = sb("x1", [P, TB, D])
        ln_gb = sb("ln_gb", [P, 2, D])
        ident = sb("ident", [P, P])
        iota = sb("iota", [P, NKEY])
        stats = sb("stats", [P, TB, 2, 6])
        moments = sb("moments", [P, TB, 2])
        rstd = sb("rstd", [P, TB, 6])

        att = ExitStack()
        xbuf = sb("xbuf", [P, KT * SEQ], F32, att)
        xT = xbuf[:, :].rearrange("p (k t) -> p k t", k=KT)
        xR = xbuf[:, :].rearrange("p (b d) -> p b d", b=TB)
        xT_hi = sb("xT_hi", [P, KT, SEQ], F32R, att)
        xT_lo = sb("xT_lo", [P, KT, SEQ], F32R, att)
        ff_w = sb("ff_w", [P, KT, HEADS], F32, att)
        ff_b = sb("ff_b", [HEADS, 1], F32, att)
        sink = sb("sink", [P, HEADS], F32, att)
        neg_sink = sb("neg_sink", [P, HEADS], F32, att)
        cst = sb("cst", [P, 4 * P + HEADS * SWA_KEYS], F32, att)
        ident_r = sb("ident_r", [P, P], F32R, att)
        mask_r = sb("mask_r", [P, 4 * P], F32R, att)
        bias_r = sb("bias_r", [P, HEADS, SWA_KEYS], F32R, att)
        ff = [sb(f"ff{i}", [HEADS, SEQ], F32, att) for i in range(5)]
        decay_r = sb("decay_r", [HEADS, 4, SEQ], F32R, att)
        decay_q = sb("decay_q", [4, 2, SEQ], F32R, att)
        decay_k = sb("decay_k", [4, 2, SEQ], F32R, att)
        qT = sb("qT", [P, SEQ], F32, att)
        kT = sb("kT", [P, SEQ], F32, att)
        vv = sb("vv", [P, TB, P], F32, att)
        swa_q = sb("swa_q", [P, SEQ], F32, att)
        swa_k = sb("swa_k", [P, SEQ], F32, att)
        swa_v = sb("swa_v", [P, TB, P], F32, att)
        probs = [sb(f"probs{i}", [P, SEQ], F32, att) for i in range(2)]
        probs_t = [sb(f"probs_t{i}", [P, 4, P], F32, att) for i in range(2)]
        row = [sb(f"row{i}", [P, 8], F32, att) for i in range(2)]
        mix_hi = sb("mix_hi", [P, KT, SEQ], F32R, att)
        mix_lo = sb("mix_lo", [P, KT, SEQ], F32R, att)
        att.close()

        x1T_hi = sb("x1T_hi", [P, KT, SEQ], F32R)
        x1T_lo = sb("x1T_lo", [P, KT, SEQ], F32R)
        onehot = [[sb(f"onehot{i}_{j}", [P, TOK_PER_TILE, NKEY], F32R) for j in range(3)] for i in range(2)]
        sel = sb("sel", [P, 3, TB, P])
        selT = sb("selT", [P, 3, SEQ])
        gateT_hi = sb("gateT_hi", [P, SEQ])
        gateT_lo = sb("gateT_lo", [P, SEQ])
        gate_r = sb("gate_r", [P, SEQ], F32R)
        gelu = [sb(f"gelu{i}", [P, SEQ]) for i in range(2)]
        route = ExitStack()
        keys = sb("keys", [P, LISTS, NKEY], F32, route)
        qh = [sb(f"qh{i}", [P, SEQ], F32, route) for i in range(2)]
        scores = sb("scores", [P, TB, LISTS, NKEY], F32, route)
        work = sb("work", [P, LISTS, NKEY], F32, route)
        best = sb("best", [P, LISTS, TOPK], F32, route)
        best_i = sb("best_i", [P, LISTS, TOPK], U32, route)
        best_f = sb("best_f", [P, LISTS, TOPK], F32, route)
        cand = sb("cand", [P, PH, TOPK * TOPK], F32, route)
        match = cand
        prod = work
        top = sb("top", [P, PH, TOPK], F32, route)
        top_i = sb("top_i", [P, PH, TOPK], U32, route)
        pos_u = sb("pos_u", [P, 2, P], U32, route)
        pos_f = sb("pos_f", [P, 2, P], F32, route)
        gsum = sb("gsum", [P, 2, TB * PH], F32, route)
        route.close()
        scat = ExitStack()
        stage = [sb(f"stage{i}", [P, ETILES, CHUNK], F32, scat) for i in range(2)]
        scat.close()
        comb = ExitStack()
        ga = [sb(f"ga{i}", [P, 4, SEQ], F32, comb) for i in range(2)]
        gg = [sb(f"gg{i}", [P, CHUNKS, 4, CHUNK], F32, comb) for i in range(2)]
        wgt = [sb(f"wgt{i}", [P, SEQ], F32, comb) for i in range(2)]
        wgt_hi = [sb(f"wgt_hi{i}", [P, SEQ], F32R, comb) for i in range(2)]
        wgt_lo = [sb(f"wgt_lo{i}", [P, SEQ], F32R, comb) for i in range(2)]
        zeros = sb("zeros", [P, SEQ], F32R, comb)
        comb.close()

        banks = ctx.enter_context(nc.psum_tensor("banks", [P, 8, 512], F32))

        raw_loaded = [sem(f"raw_loaded{i}") for i in range(RAW_SLOTS)]
        hi_ready = sem("hi_ready")
        lo_ready = sem("lo_ready")
        tile_used = sem("tile_used")
        xT_loaded = sem("xT_loaded")
        small_loaded = sem("small_loaded")
        xR_loaded = sem("xR_loaded")
        ln_loaded = sem("ln_loaded")
        xT_split = sem("xT_split")
        consts_ready = sem("consts_ready")
        ff_ready = sem("ff_ready")
        ff_step = sem("ff_step")
        decay_ready = sem("decay_ready")
        decay_stored = sem("decay_stored")
        decay_loaded = sem("decay_loaded")
        proj_copied = sem("proj_copied")
        logits_ready = sem("logits_ready")
        max_step = sem("max_step")
        max_ready = sem("max_ready")
        exp_ready = sem("exp_ready")
        norm_step = sem("norm_step")
        probs_ready = sem("probs_ready")
        turned = sem("turned")
        turned_copied = sem("turned_copied")
        head_mixed = sem("head_mixed")
        mix_hi_ready = sem("mix_hi_ready")
        mix_lo_ready = sem("mix_lo_ready")
        ln_step = sem("ln_step")
        sqrt_ready = sem("sqrt_ready")
        norm_chain = sem("norm_chain")
        x1_ready = sem("x1_ready")
        x1_turned = sem("x1_turned")
        x1T_hi_ready = sem("x1T_hi_ready")
        x1T_lo_ready = sem("x1T_lo_ready")
        keys_loaded = sem("keys_loaded")
        qh_ready = sem("qh_ready")
        scored = sem("scored")
        scores_ready = sem("scores_ready")
        route_step = sem("route_step")
        route_tick = sem("route_tick")
        gate_exp = sem("gate_exp")
        gate_step = sem("gate_step")
        gates_ready = sem("gates_ready")
        sel_turned = sem("sel_turned")
        selT_ready = sem("selT_ready")
        gelu_ready = sem("gelu_ready")
        gelu_stored = [sem(f"gelu_stored{i}") for i in range(2)]
        onehot_ready = sem("onehot_ready")
        scattered = sem("scattered")
        staged = sem("staged")
        g_stored = [sem(f"g_stored{i}") for i in range(2)]
        comb_loaded = [sem(f"comb_loaded{i}") for i in range(2)]
        wgt_ready = sem("wgt_ready")
        wgt_hi_ready = sem("wgt_hi_ready")
        wgt_lo_ready = sem("wgt_lo_ready")
        zeros_ready = sem("zeros_ready")
        combined = sem("combined")
        y_ready = sem("y_ready")
        out_stored = sem("out_stored")

        def wait(eng, s, value):
            if not (isinstance(value, int) and value <= 0):
                eng.wait_ge(s, value)


        def load_tile(eng, c, it, src):
            wait(eng, lo_ready, 4 * it + (c - RAW_SLOTS + 1))
            eng.dma_start(raw[:, c % RAW_SLOTS, :], src).then_inc(raw_loaded[c % RAW_SLOTS], 16)

        def split_hi(act, c, it):
            wait(act, raw_loaded[c % RAW_SLOTS], 16 * it + 16 * (c // RAW_SLOTS + 1))
            wait(act, tile_used, 4 * it + (c - PART_SLOTS + 1))
            act.activation(hi[c % PART_SLOTS][:, :], raw[:, c % RAW_SLOTS, :], ACT.Copy).then_inc(hi_ready, 1)

        def split_lo(eng, c, it):
            wait(eng, hi_ready, 4 * it + (c + 1))
            eng.tensor_tensor(lo[c % PART_SLOTS][:, :], raw[:, c % RAW_SLOTS, :],
                              hi[c % PART_SLOTS][:, :].bitcast(F32), ALU.subtract).then_inc(lo_ready, 1)

        def units():
            for a in range(2):
                for qb in range(TB):
                    yield "fox", a, qb, 0, qb + 1
            for a in range(2):
                for qb in range(TB):
                    yield "swa", a, qb, max(qb - 1, 0), min(qb, 1) + 1

        UNITS = list(units())
        NU = len(UNITS)
        SWA_UNITS = NU // 2

        def count_swa(u):
            return sum(1 for k in UNITS[:u] if k[0] == "swa")

        block = ctx.enter_context(nc.Block())

        @block.sync
        def _(sp):
            sp.dma_start(xT, x_t).then_inc(xT_loaded, 16)
            for c in range(S_LOOP):
                load_tile(sp, c, 0, w1[c])
            sp.dma_start(cst[:, :], consts[:, 0:4 * P + HEADS * SWA_KEYS]).then_inc(small_loaded, 16)
            sp.dma_start(ident[:, :], consts[:, 4 * P + HEADS * SWA_KEYS:5 * P + HEADS * SWA_KEYS]).then_inc(small_loaded, 16)
            sp.dma_start(iota[:, :], consts[:, 5 * P + HEADS * SWA_KEYS:]).then_inc(small_loaded, 16)
            sp.dma_start(ff_w[:, :, :], w_ff).then_inc(small_loaded, 16)
            sp.dma_start(ff_b[:, :], b_f).then_inc(small_loaded, 16)
            sp.dma_start(sink[:, :], sinks).then_inc(small_loaded, 16)
            sp.dma_start(ln_gb[:, :, :], ln_par[:, 0:2, :]).then_inc(ln_loaded, 16)
            for c in range(S_LOOP, S_LOOP + 4):
                load_tile(sp, c, 0, w1[c])
            with sp.Fori(1, PAIRS) as j:
                for k in range(4):
                    load_tile(sp, S_LOOP + k, j, w1[4 * j + (S_LOOP + k)])
            sp.wait_ge(xT_split, 2)
            sp.wait_ge(ff_ready, 1)
            sp.dma_start(xR, x_rows).then_inc(xR_loaded, 16)
            for c in range(S_WOUT, S_PQ):
                load_tile(sp, c, 0, w1[c])
            for c in range(S_PQ, S_PQ + 4):
                load_tile(sp, c, 0, w_pq[c - S_PQ])
            sp.wait_ge(x1T_lo_ready, TB)
            sp.dma_start(keys[:, :, :], keys_t).then_inc(keys_loaded, 16)
            sp.dma_start(ln_gb[:, :, :], ln_par[:, 2:4, :]).then_inc(ln_loaded, 16)
            with sp.Fori(1, LISTS // 4) as i:
                for k in range(4):
                    load_tile(sp, S_PQ + k, i, w_pq[4 * i + k])

            def store_gelu(slot, n_it, k, value):
                sp.wait_ge(gelu_ready, value)
                sp.dma_start(a_dram[n_it, :, k, :], gelu[slot][:, :]).then_inc(gelu_stored[slot], 16)

            for k in range(4):
                load_tile(sp, S_U + k, 0, u_t[k])

            def tiles_and_stores(it):
                for k in range(4):
                    load_tile(sp, S_U + 4 + k, it, u_t[4 * it + (4 + k)])
                    store_gelu(k % 2, it, k, 4 * it + (k + 1))

            with sp.Fori(0, A_PRE // 4) as it:
                tiles_and_stores(it)
            with sp.Fori(0, CHUNKS // 2) as o:
                for half in range(2):
                    for q in range(TILES_PER_CHUNK // 4):
                        tiles_and_stores(4 * o + (A_PRE // 4 + 2 * half + q))
                    sp.wait_ge(staged, 32 * o + 16 * (half + 1))
                    sp.dma_start(g_dram[2 * o + half], stage[half][:, :, :]).then_inc(g_stored[half], 16)
            for it in range((A_PRE + A_MID) // 4, ETILES // 4 - 1):
                tiles_and_stores(it)
            for k in range(4):
                load_tile(sp, S_V + k, 0, v_tab[k])
                store_gelu(k % 2, ETILES // 4 - 1, k, ETILES - 4 + k + 1)
            for half in range(2):
                sp.wait_ge(gelu_stored[half], 16 * ETILES // 2)
                sp.wait_ge(g_stored[half], 16 * CHUNKS // 2)

            def load_group(g, slot):
                sp.dma_start(ga[slot][:, :, :], a_dram[g]).then_inc(comb_loaded[slot], 16)
                sp.dma_start(gg[slot][:, :, :, :],
                             g_dram[:, :, bass.ds(4 * g, 4), :].rearrange("c p n t -> p c n t")
                             ).then_inc(comb_loaded[slot], 16)

            load_group(0, 0)
            load_group(1, 1)
            for k in range(4):
                load_tile(sp, S_V + 4 + k, 0, v_tab[4 + k])
            with sp.Fori(1, ETILES // 8) as i:
                for slot in range(2):
                    sp.wait_ge(wgt_ready, 8 * i + (4 * slot - 4))
                    load_group(2 * i + slot, slot)
                    for k in range(4):
                        load_tile(sp, S_V + 4 * slot + k, 2 * i, v_tab[8 * i + (4 * slot + k)])
            for b in range(TB):
                sp.wait_ge(y_ready, b + 1)
                sp.dma_start(out[bass.ts(b, P), :], x1[:, b, :]).then_inc(out_stored, 16)
            sp.wait_ge(out_stored, 16 * TB)

        @block.gpsimd
        def _(pool):
            pool.memset(decay_q[:, :, :].bitcast(F32), 1.0).then_inc(decay_ready, 1)
            pool.memset(decay_k[:, :, :].bitcast(F32), 1.0).then_inc(decay_ready, 1)
            for c in range(S_LOOP):
                split_lo(pool, c, 0)
            pool.wait_ge(decay_ready, 6)
            pool.dma_start(c_dram.rearrange("r h t -> h r t"), decay_r[:, :, :]).then_inc(decay_stored, 16)
            pool.wait_ge(decay_stored, 16)

            def load_decay(j):
                pool.dma_start(decay_q[2:4, :, :], c_dram[0:2, bass.ds(2 * j, 2), :]).then_inc(decay_loaded, 16)
                pool.dma_start(decay_k[0:2, :, :], c_dram[2:4, bass.ds(2 * j, 2), :]).then_inc(decay_loaded, 16)

            load_decay(0)
            for k in range(2):
                split_lo(pool, S_LOOP + k, 0)
            with pool.Fori(0, PAIRS - 1) as j:
                for k in range(2, 6):
                    split_lo(pool, S_LOOP + k, j)
                pool.wait_ge(logits_ready, NU * j + SWA_UNITS)
                load_decay(j + 1)
            for c in range(S_WOUT - 2, S_PQ):
                split_lo(pool, c, 0)
            with pool.Fori(0, (N_TILES - S_PQ) // 8) as it:
                for k in range(8):
                    split_lo(pool, S_PQ + k, 2 * it)

        @block.scalar
        def _(act):
            act.wait_ge(xT_loaded, 16)
            act.activation(xT_hi[:, :, :], xT, ACT.Copy).then_inc(xT_split, 1)
            for c in range(S_LOOP):
                split_hi(act, c, 0)
            act.wait_ge(small_loaded, 96)
            act.activation(mask_r[:, :], cst[:, 0:4 * P], ACT.Copy).then_inc(consts_ready, 1)
            act.activation(bias_r[:, :, :], cst[:, 4 * P:].rearrange("p (h k) -> p h k", h=HEADS),
                           ACT.Copy).then_inc(consts_ready, 1)
            act.activation(ident_r[:, :], ident[:, :], ACT.Copy).then_inc(consts_ready, 1)
            act.wait_ge(ff_ready, 1)
            act.activation(ff[0][:, :], banks[0:HEADS, 2, :], ACT.Identity, bias=ff_b[:, :]).then_inc(ff_step, 1)
            act.wait_ge(ff_step, 1)
            act.activation(ff[1][:, :], ff[0][:, :], ACT.Abs).then_inc(ff_step, 1)
            act.wait_ge(ff_step, 2)
            act.activation(ff[2][:, :], ff[1][:, :], ACT.Exp, scale=-1.0).then_inc(ff_step, 1)
            act.wait_ge(ff_step, 3)
            act.activation(ff[3][:, :], ff[2][:, :], ACT.Ln, bias=1.0).then_inc(ff_step, 1)

            def copy_proj(value, dst, bank, scale=1.0):
                act.wait_ge(tile_used, value)
                act.activation(dst, banks[:, bank, :], ACT.Copy, scale=scale).then_inc(proj_copied, 1)

            copy_proj(1, swa_k[:, :], 0)
            copy_proj(2, swa_v[:, :, :].rearrange("p b d -> p (b d)"), 1)
            for k in range(2):
                split_hi(act, S_LOOP + k, 0)

            def pair(j, last):
                copy_proj(4 * j + (S_LOOP + 1), qT[:, :], 0, HD ** -0.5)
                split_hi(act, S_LOOP + 2, j)
                copy_proj(4 * j + (S_LOOP + 2), kT[:, :], 1)
                split_hi(act, S_LOOP + 3, j)
                copy_proj(4 * j + (S_LOOP + 3), vv[:, :, :].rearrange("p b d -> p (b d)"), 0)
                split_hi(act, S_LOOP + 4, j)
                copy_proj(4 * j + (S_LOOP + 4), swa_q[:, :], 1, HD ** -0.5)
                split_hi(act, S_LOOP + 5, j)

                def exponentials(u):
                    kind, a, qb, k0, nk = UNITS[u]
                    act.wait_ge(max_ready, NU * j + (u + 1))
                    r = row[u % 2]
                    ins = act.activation(probs[u % 2][:, 0:nk * P], banks[:, 2 + u % 2, 0:nk * P], ACT.Exp,
                                         bias=r[:, 1:2], accum_out=r[:, 2:3])
                    if kind == "swa":
                        ins = act.activation(r[:, 3:4], sink[:, bass.ds(2 * j + a, 1)], ACT.Exp, bias=r[:, 1:2])
                    ins.then_inc(exp_ready, 1)

                def copy_turned(u):
                    kind, a, qb, k0, nk = UNITS[u]
                    act.wait_ge(turned, NU * j + (u + 1))
                    if u >= 2 or not isinstance(j, int):
                        act.wait_ge(head_mixed, NU * j + (u - 1))
                    act.activation(probs_t[u % 2][:, 0:nk, :],
                                   banks[:, 4 + u % 2, 0:nk * P].rearrange("p (k q) -> p k q", k=nk),
                                   ACT.Copy).then_inc(turned_copied, 1)

                for u in range(NU + 2):
                    if u < NU:
                        exponentials(u)
                    if 1 <= u <= NU:
                        copy_turned(u - 1)
                    if u in (SWA_UNITS + 1, NU + 1):
                        g = 0 if u < NU else 1
                        act.wait_ge(head_mixed, NU * j + SWA_UNITS * (g + 1))
                        act.activation(mix_hi[:, bass.ds(j + PAIRS * g, 1), :].rearrange("p o t -> p (o t)"),
                                       banks[:, 6 + g, :], ACT.Copy).then_inc(mix_hi_ready, 1)

            pair(0, False)
            with act.Fori(1, PAIRS) as j:
                pair(j, False)
            for c in range(S_WOUT + 2, S_PQ + 1 + 1):
                split_hi(act, c, 0)

            for b in range(TB):
                act.wait_ge(ln_step, 3 * (b + 1))
                act.activation(rstd[:, b, 1:2], rstd[:, b, 0:1], ACT.Sqrt).then_inc(sqrt_ready, 1)
            for b in range(TB):
                act.wait_ge(x1_turned, b + 1)
                act.activation(x1T_hi[:, :, bass.ts(b, P)],
                               banks[:, 2 * b:2 * b + 2, :].rearrange("p h (k t) -> p (h k) t", t=P),
                               ACT.Copy).then_inc(x1T_hi_ready, 1)

            def copy_query(l, it):
                act.wait_ge(tile_used, 4 * it + (S_PQ + l + 1))
                wait(act, scored, 4 * it + (l - 1))
                act.activation(qh[l % 2][:, :], banks[:, l % 2, :], ACT.Copy).then_inc(qh_ready, 1)

            def copy_scores(l, it):
                act.wait_ge(scored, 4 * it + (l + 1))
                act.activation(scores[:, :, bass.ds(4 * it + l, 1), :].rearrange("p b o n -> p b (o n)"),
                               banks[:, 2 + l % 2, :].rearrange("p (b n) -> p b n", b=TB),
                               ACT.Copy).then_inc(scores_ready, 1)

            def query_group(it):
                for l in range(4):
                    copy_query(l, it)
                    split_hi(act, S_PQ + 2 + l, it)
                    copy_scores(l, it)

            query_group(0)
            with act.Fori(1, LISTS // 4) as it:
                query_group(it)

            def gelu_tile(k, it, first=False):
                act.wait_ge(tile_used, 4 * it + (S_U + k + 1))
                if not first:
                    act.wait_ge(gelu_stored[k % 2], 32 * it + 16 * (k // 2))
                act.activation(gelu[k % 2][:, :], banks[:, k % 2, :], ACT.Gelu).then_inc(gelu_ready, 1)
                split_hi(act, S_U + 2 + k, it)

            for k in range(4):
                gelu_tile(k, 0, first=k < 2)
            with act.Fori(1, A_PRE // 4) as it:
                for k in range(4):
                    gelu_tile(k, it)

            act.wait_ge(route_step, ROUTE_STEPS * TB)
            act.activation(sel[:, 2, :, :], sel[:, 2, :, :], ACT.Exp).then_inc(gate_exp, 1)
            for m in range(3):
                act.wait_ge(sel_turned, m + 1)
                act.activation(selT[:, m, :], banks[:, 2 + m, :], ACT.Copy).then_inc(selT_ready, 1)

            def stage_gates(chunk_half, o, tile, first):
                for g in range(2):
                    n = 2 * tile + g
                    act.wait_ge(scattered, 32 * o + (16 * chunk_half + n + 1))
                    if tile == 0 and g == 0 and not first:
                        act.wait_ge(g_stored[chunk_half], 16 * o)
                    t0 = tile * TOK_PER_TILE + 4 * g
                    act.activation(stage[chunk_half][:, :, t0:t0 + 4].rearrange("p n t -> p t n"),
                                   banks[:, 2 + g, :].rearrange("p (t n) -> p t n", t=4),
                                   ACT.Copy).then_inc(staged, 1)

            def two_chunks(o, first):
                for half in range(2):
                    for tile in range(TILES_PER_CHUNK):
                        gelu_tile(tile % 4, 4 * o + (A_PRE // 4 + 2 * half + tile // 4))
                        stage_gates(half, o, tile, first)

            two_chunks(0, True)
            with act.Fori(1, CHUNKS // 2) as o:
                two_chunks(o, False)
            for it in range((A_PRE + A_MID) // 4, ETILES // 4):
                for k in range(4):
                    gelu_tile(k, it)

            def weight_hi(k, it, first=False):
                act.wait_ge(wgt_ready, 4 * it + (k + 1))
                if not first:
                    act.wait_ge(tile_used, 4 * it + (S_V + k - 1))
                act.activation(wgt_hi[k % 2][:, :], wgt[k % 2][:, :], ACT.Copy).then_inc(wgt_hi_ready, 1)

            weight_hi(0, 0, True)
            weight_hi(1, 0, True)
            with act.Fori(0, ETILES // 8 - 1) as i:
                for k in range(8):
                    split_hi(act, S_V + 2 + k, 2 * i)
                    weight_hi(2 + k, 2 * i)
            for k in range(6):
                split_hi(act, N_TILES - 6 + k, 0)
                weight_hi(ETILES - 6 + k, 0)
            for b in range(TB):
                act.wait_ge(ln_step, 3 * (TB + b + 1))
                act.activation(rstd[:, b, 1:2], rstd[:, b, 0:1], ACT.Sqrt).then_inc(sqrt_ready, 1)

        @block.vector
        def _(dve):
            dve.wait_ge(xT_split, 1)
            dve.tensor_tensor(xT_lo[:, :, :], xT, xT_hi[:, :, :].bitcast(F32), ALU.subtract).then_inc(xT_split, 1)
            dve.wait_ge(small_loaded, 96)
            dve.tensor_scalar(neg_sink[:, :], sink[:, :], -1.0, None, ALU.mult).then_inc(consts_ready, 1)
            dve.memset(ff[4][:, :], 1.0).then_inc(max_step, 1)
            dve.wait_ge(ff_step, 4)
            dve.scalar_tensor_tensor(ff[1][:, :], ff[0][:, :], 0.0, ff[3][:, :], ALU.min, ALU.subtract).then_inc(ff_step, 1)
            dve.wait_ge(ff_step, 5)
            dve.wait_ge(max_step, 1)
            dve.tensor_tensor_scan(ff[2][:, :], ff[4][:, :], ff[1][:, :], 0.0, ALU.mult, ALU.add).then_inc(ff_step, 1)
            dve.wait_ge(ff_step, 6)
            dve.tensor_copy(decay_r[:, 0, :], ff[2][:, :]).then_inc(decay_ready, 1)
            dve.wait_ge(decay_ready, 3)
            dve.tensor_tensor(decay_r[:, 1, :], ff[2][:, :], decay_r[:, 0, :].bitcast(F32), ALU.subtract).then_inc(decay_ready, 1)
            dve.tensor_scalar(decay_r[:, 2, :], decay_r[:, 0, :].bitcast(F32), -1.0, None, ALU.mult).then_inc(decay_ready, 1)
            dve.wait_ge(decay_ready, 4)
            dve.tensor_scalar(decay_r[:, 3, :], decay_r[:, 1, :].bitcast(F32), -1.0, None, ALU.mult).then_inc(decay_ready, 1)

            def pair(j, first):
                def maximum(u):
                    kind, a, qb, k0, nk = UNITS[u]
                    r = row[u % 2]
                    dve.wait_ge(logits_ready, NU * j + (u + 1))
                    src = banks[:, 2 + u % 2, 0:nk * P]
                    if kind == "fox":
                        dve.tensor_reduce(r[:, 1:2], src, AX_X, ALU.max, negate=True).then_inc(max_ready, 1)
                    else:
                        dve.tensor_reduce(r[:, 0:1], src, AX_X, ALU.max, negate=True).then_inc(max_step, 1)
                        dve.wait_ge(max_step, SWA_UNITS * j + (count_swa(u) + 2))
                        dve.tensor_tensor(r[:, 1:2], r[:, 0:1], neg_sink[:, bass.ds(2 * j + a, 1)],
                                          ALU.min).then_inc(max_ready, 1)

                def normalise(u):
                    kind, a, qb, k0, nk = UNITS[u]
                    r = row[u % 2]
                    dve.wait_ge(exp_ready, NU * j + (u + 1))
                    steps = (NU + SWA_UNITS) * j + (u + count_swa(u))
                    if kind == "fox":
                        dve.reciprocal(r[:, 4:5], r[:, 2:3]).then_inc(norm_step, 1)
                        dve.wait_ge(norm_step, steps + 1)
                    else:
                        dve.tensor_tensor(r[:, 5:6], r[:, 2:3], r[:, 3:4], ALU.add).then_inc(norm_step, 1)
                        dve.wait_ge(norm_step, steps + 1)
                        dve.reciprocal(r[:, 4:5], r[:, 5:6]).then_inc(norm_step, 1)
                        dve.wait_ge(norm_step, steps + 2)
                    dve.tensor_scalar(probs[u % 2][:, 0:nk * P], probs[u % 2][:, 0:nk * P], r[:, 4:5], None,
                                      ALU.mult).then_inc(probs_ready, 1)

                for u in range(NU + 2):
                    if u < NU:
                        maximum(u)
                    if 1 <= u <= NU:
                        normalise(u - 1)
                    if u in (SWA_UNITS + 1, NU + 1):
                        g = 0 if u < NU else 1
                        dve.wait_ge(mix_hi_ready, 2 * j + (g + 1))
                        s = bass.ds(j + PAIRS * g, 1)
                        dve.tensor_tensor(mix_lo[:, s, :].rearrange("p o t -> p (o t)"), banks[:, 6 + g, :],
                                          mix_hi[:, s, :].rearrange("p o t -> p (o t)").bitcast(F32),
                                          ALU.subtract).then_inc(mix_lo_ready, 1)

            pair(0, True)
            with dve.Fori(1, PAIRS) as j:
                pair(j, False)

            def layer_norm(b, rows, n, done):
                base = 3 * n
                for h in range(2):
                    ins = dve.bn_stats(stats[:, b, h, :], rows[:, bass.ts(h, 512)])
                ins.then_inc(ln_step, 1)
                dve.wait_ge(ln_step, base + 1)
                dve.bn_aggr(moments[:, b, :], stats[:, b, :, :]).then_inc(ln_step, 1)
                dve.wait_ge(ln_step, base + 2)
                dve.tensor_scalar(rstd[:, b, 0:1], moments[:, b, 1:2], EPS, None, ALU.add).then_inc(ln_step, 1)

            ln_chain = [0]

            def chained(ins):
                ins.then_inc(norm_chain, 1)
                ln_chain[0] += 1
                dve.wait_ge(norm_chain, ln_chain[0])

            def finish_norm(b, rows, n, done):
                dve.wait_ge(sqrt_ready, n + 1)
                v, s, r0, t, r1 = (rstd[:, b, i:i + 1] for i in range(5))
                chained(dve.reciprocal(r0, s))
                chained(dve.scalar_tensor_tensor(t, r0, v, r0, ALU.mult, ALU.mult))
                chained(dve.tensor_scalar(t, t, -0.5, 1.5, ALU.mult, ALU.add))
                chained(dve.tensor_tensor(r1, r0, t, ALU.mult))
                chained(dve.tensor_scalar(rows, rows, moments[:, b, 0:1], r1, ALU.subtract, ALU.mult))
                chained(dve.tensor_tensor(rows, rows, ln_gb[:, 0, :], ALU.mult))
                dve.tensor_tensor(rows, rows, ln_gb[:, 1, :], ALU.add).then_inc(done, 1)

            dve.wait_ge(xR_loaded, 16)
            dve.wait_ge(ln_loaded, 16)
            dve.wait_ge(tile_used, S_PQ)
            for b in range(TB):
                chained(dve.scalar_tensor_tensor(x1[:, b, :], xR[:, b, :], ALPHA,
                                                 banks[:, 2 * b:2 * b + 2, :].rearrange("p h n -> p (h n)"),
                                                 ALU.mult, ALU.add))
                layer_norm(b, x1[:, b, :], b, None)
            for b in range(TB):
                finish_norm(b, x1[:, b, :], b, x1_ready)
            for b in range(TB):
                dve.wait_ge(x1T_hi_ready, b + 1)
                dve.tensor_tensor(x1T_lo[:, :, bass.ts(b, P)],
                                  banks[:, 2 * b:2 * b + 2, :].rearrange("p h (k t) -> p (h k) t", t=P),
                                  x1T_hi[:, :, bass.ts(b, P)].bitcast(F32), ALU.subtract).then_inc(x1T_lo_ready, 1)

            def route_block(b):
                n = [0]

                def begin():
                    wait(dve, route_step, ROUTE_STEPS * b + n[0])
                    dve.sem_inc(route_tick, 1)

                def step(ins):
                    ins.then_inc(route_step, 1)
                    n[0] += 1

                def top16(vals, idx, src, count):
                    for l in range(count):
                        ins = dve.max(vals[:, l, 0:8], src[:, l, :])
                    step(ins)
                    begin()
                    for l in range(count):
                        ins = dve.max_index(idx[:, l, 0:8], vals[:, l, 0:8], src[:, l, :])
                    step(ins)
                    begin()
                    for l in range(count):
                        ins = dve.match_replace(src[:, l, :], vals[:, l, 0:8], src[:, l, :], NEG_MAX)
                    step(ins)
                    begin()
                    for l in range(count):
                        ins = dve.max(vals[:, l, 8:16], src[:, l, :])
                    step(ins)
                    begin()
                    for l in range(count):
                        ins = dve.max_index(idx[:, l, 8:16], vals[:, l, 8:16], src[:, l, :])
                    step(ins)
                    begin()

                begin()
                step(dve.tensor_copy(work[:, :, :], scores[:, bass.ds(b, 1), :, :].rearrange("p o l n -> p (o l) n")))
                begin()
                top16(best, best_i, work, LISTS)
                step(dve.tensor_copy(best_f[:, :, :], best_i[:, :, :]))
                halves = best[:, :, :].rearrange("p (h s) k -> p h s k", s=2)
                step(dve.tensor_tensor(cand[:, :, :].rearrange("p h (i j) -> p h i j", j=TOPK),
                                       halves[:, :, 0, :].unsqueeze(3).to_broadcast([P, PH, TOPK, TOPK]),
                                       halves[:, :, 1, :].unsqueeze(2).to_broadcast([P, PH, TOPK, TOPK]), ALU.add))
                begin()
                top16(top, top_i, cand, PH)
                flat_i = top_i[:, :, :].rearrange("p h k -> p (h k)")
                step(dve.tensor_scalar(pos_u[:, 0, :], flat_i, 4, None, ALU.logical_shift_right))
                step(dve.tensor_scalar(pos_u[:, 1, :], flat_i, TOPK - 1, None, ALU.bitwise_and))
                begin()
                step(dve.tensor_copy(pos_f[:, :, :], pos_u[:, :, :]))
                step(dve.tensor_tensor(sel[:, 2, bass.ds(b, 1), :].rearrange("p o (h k) -> p (o h) k", k=TOPK), top[:, :, :],
                                       top[:, :, 0:1].to_broadcast([P, PH, TOPK]), ALU.subtract))
                begin()
                ids = best_f[:, :, :].rearrange("p (h s) k -> p h s k", s=2)
                for s in range(2):
                    step(dve.tensor_tensor(match[:, :, :].rearrange("p h (k j) -> p (h k) j", j=TOPK),
                                           pos_f[:, s, :].unsqueeze(2).to_broadcast([P, P, TOPK]),
                                           iota[:, 0:TOPK].unsqueeze(1).to_broadcast([P, P, TOPK]), ALU.is_equal))
                    begin()
                    step(dve.tensor_tensor(prod[:, :, :].rearrange("p (h a) (k j) -> p h (a k) j", a=2, j=TOPK),
                                           match[:, :, :].rearrange("p h (k j) -> p h k j", j=TOPK),
                                           ids[:, :, s, :].unsqueeze(2).to_broadcast([P, PH, TOPK, TOPK]), ALU.mult))
                    begin()
                    ins = dve.tensor_reduce(sel[:, s, bass.ds(b, 1), :].rearrange("p o n -> p (o n)"),
                                            prod[:, :, :].rearrange("p l (k j) -> p (l k) j", j=TOPK), AX_X, ALU.add)
                    step(ins)
                    begin()
                ROUTE_SEEN[0] = n[0]

            ROUTE_SEEN = [0]
            dve.wait_ge(scores_ready, LISTS)
            with dve.Fori(0, TB) as b:
                route_block(b)
            assert ROUTE_SEEN[0] == ROUTE_STEPS, ROUTE_SEEN

            gates = sel[:, 2, :, :].rearrange("p b (h k) -> p (b h) k", k=TOPK)
            dve.wait_ge(gate_exp, 1)
            dve.tensor_reduce(gsum[:, 0, :], gates, AX_X, ALU.add).then_inc(gate_step, 1)
            dve.wait_ge(gate_step, 1)
            dve.reciprocal(gsum[:, 1, :], gsum[:, 0, :]).then_inc(gate_step, 1)
            dve.wait_ge(gate_step, 2)
            dve.tensor_tensor(gates, gates, gsum[:, 1, :].unsqueeze(2).to_broadcast([P, TB * PH, TOPK]),
                              ALU.mult).then_inc(gates_ready, 1)
            dve.wait_ge(selT_ready, 3)
            dve.tensor_copy(gate_r[:, :], selT[:, 2, :]).then_inc(gate_step, 1)
            dve.wait_ge(gate_step, 3)
            dve.tensor_copy(gateT_hi[:, :], gate_r[:, :].bitcast(F32)).then_inc(gate_step, 1)
            dve.tensor_tensor(gateT_lo[:, :], selT[:, 2, :], gate_r[:, :].bitcast(F32), ALU.subtract).then_inc(gate_step, 1)
            dve.wait_ge(gate_step, 5)

            def one_hots(tile, o, first):
                slot = tile % 2
                if not first:
                    dve.wait_ge(scattered, 32 * o + (2 * tile - 2))
                for k in range(TOK_PER_TILE):
                    t = bass.ds(2 * CHUNK * o + (TOK_PER_TILE * tile + k), 1)
                    dve.tensor_scalar(onehot[slot][0][:, k, :], iota[:, :], selT[:, 1, t], None, ALU.is_equal)
                    dve.tensor_scalar(onehot[slot][1][:, k, :], iota[:, :], selT[:, 0, t], gateT_hi[:, t],
                                      ALU.is_equal, ALU.mult)
                    ins = dve.tensor_scalar(onehot[slot][2][:, k, :], iota[:, :], selT[:, 0, t], gateT_lo[:, t],
                                            ALU.is_equal, ALU.mult)
                ins.then_inc(onehot_ready, 1)

            for tile in range(2 * TILES_PER_CHUNK):
                one_hots(tile, 0, tile < 2)
            with dve.Fori(1, CHUNKS // 2) as o:
                for tile in range(2 * TILES_PER_CHUNK):
                    one_hots(tile, o, False)

            dve.wait_ge(g_stored[0], 16 * CHUNKS // 2)
            dve.wait_ge(g_stored[1], 16 * CHUNKS // 2)
            dve.memset(zeros[:, :].bitcast(F32), 0.0).then_inc(zeros_ready, 1)

            def weights(k, it, group, it_group, first):
                if k % 4 == 0:
                    dve.wait_ge(comb_loaded[group], 32 * it_group + 32)
                if not first:
                    dve.wait_ge(wgt_lo_ready, 4 * it + (k - 1))
                dve.tensor_tensor(wgt[k % 2][:, :].rearrange("p (c t) -> p c t", c=CHUNKS),
                                  ga[group][:, k % 4, :].rearrange("p (c t) -> p c t", c=CHUNKS),
                                  gg[group][:, :, k % 4, :], ALU.mult).then_inc(wgt_ready, 1)

            def weight_lo(k, it):
                dve.wait_ge(wgt_hi_ready, 4 * it + (k + 1))
                dve.tensor_tensor(wgt_lo[k % 2][:, :], wgt[k % 2][:, :], wgt_hi[k % 2][:, :].bitcast(F32),
                                  ALU.subtract).then_inc(wgt_lo_ready, 1)

            for k in range(8):
                weights(k, 0, k // 4, 0, k < 2)
                weight_lo(k, 0)
            with dve.Fori(1, ETILES // 8) as i:
                for k in range(8):
                    weights(k, 2 * i, k // 4, i, False)
                    weight_lo(k, 2 * i)

            dve.wait_ge(ln_loaded, 32)
            dve.wait_ge(combined, 1)
            for b in range(TB):
                chained(dve.scalar_tensor_tensor(x1[:, b, :], x1[:, b, :], ALPHA,
                                                 banks[:, 2 * b:2 * b + 2, :].rearrange("p h n -> p (h n)"),
                                                 ALU.mult, ALU.add))
                layer_norm(b, x1[:, b, :], TB + b, None)
            for b in range(TB):
                finish_norm(b, x1[:, b, :], TB + b, y_ready)

        @block.tensor
        def _(pe):
            pe.wait_ge(xT_loaded, 16)
            pe.wait_ge(small_loaded, 96)
            for k in range(KT):
                ins = pe.matmul(banks[0:HEADS, 2, :], ff_w[:, k, :], xT[:, k, :], start=(k == 0), stop=(k == KT - 1))
            ins.then_inc(ff_ready, 1)
            pe.wait_ge(xT_split, 2)

            def features(c, it, bank, hiT, loT):
                pe.wait_ge(lo_ready, 4 * it + (c + 1))
                h, l = hi[c % PART_SLOTS], lo[c % PART_SLOTS]
                for k in range(KT):
                    s = bass.ts(k, P)
                    pe.matmul(banks[:, bank, :], h[:, s], hiT[:, k, :], start=(k == 0), stop=False)
                    pe.matmul(banks[:, bank, :], h[:, s], loT[:, k, :], start=False, stop=False)
                    ins = pe.matmul(banks[:, bank, :], l[:, s], hiT[:, k, :], start=False, stop=(k == KT - 1))
                ins.then_inc(tile_used, 1)

            def values(c, it, bank):
                pe.wait_ge(lo_ready, 4 * it + (c + 1))
                h, l = hi[c % PART_SLOTS], lo[c % PART_SLOTS]
                for b in range(TB):
                    o = banks[:, bank, bass.ts(b, P)]
                    for k in range(KT):
                        s = bass.ts(k, P)
                        pe.matmul(o, xT_hi[:, k, bass.ts(b, P)], h[:, s], start=(k == 0), stop=False)
                        pe.matmul(o, xT_hi[:, k, bass.ts(b, P)], l[:, s], start=False, stop=False)
                        ins = pe.matmul(o, xT_lo[:, k, bass.ts(b, P)], h[:, s], start=False, stop=(k == KT - 1))
                ins.then_inc(tile_used, 1)

            features(0, 0, 0, xT_hi, xT_lo)
            values(1, 0, 1)
            pe.wait_ge(consts_ready, 4)

            def pair(j, first):
                pe.wait_ge(proj_copied, 4 * j + 1)
                features(S_LOOP, j, 0, xT_hi, xT_lo)
                pe.wait_ge(proj_copied, 4 * j + 2)
                features(S_LOOP + 1, j, 1, xT_hi, xT_lo)
                pe.wait_ge(proj_copied, 4 * j + 3)
                values(S_LOOP + 2, j, 0)
                pe.wait_ge(proj_copied, 4 * j + 4)
                features(S_LOOP + 3, j, 1, xT_hi, xT_lo)
                pe.wait_ge(proj_copied, 4 * j + 6)
                pe.wait_ge(decay_loaded, 32 * j + 32)
                if not first:
                    pe.wait_ge(mix_lo_ready, 2 * j)

                def logits(u):
                    kind, a, qb, k0, nk = UNITS[u]
                    hs = slice(a * HD, (a + 1) * HD)
                    qs = bass.ts(qb, P)
                    o = banks[:, 2 + u % 2, 0:nk * P]
                    if u >= 2 or not first:
                        pe.wait_ge(exp_ready, NU * j + (u - 1))
                    elif first and u == 0:
                        pe.wait_ge(ff_step, 4)
                    if kind == "fox":
                        pe.matmul(o, qT[hs, qs], kT[hs, 0:nk * P], start=True, stop=False)
                        pe.matmul(o, decay_q[:, a, qs], decay_k[:, a, 0:nk * P], start=False, stop=False)
                        pe.matmul(o, ident_r[:, :], mask_r[:, (4 - nk) * P:], start=False, stop=True).then_inc(logits_ready, 1)
                    else:
                        pe.matmul(o, swa_q[hs, qs], swa_k[hs, k0 * P:(k0 + nk) * P], start=True, stop=False)
                        pe.matmul(o, ident_r[:, :],
                                  bias_r[:, bass.ds(2 * j + a, 1), (2 - nk) * P:].rearrange("p o k -> p (o k)"),
                                  start=False, stop=True).then_inc(logits_ready, 1)

                def turn(u):
                    kind, a, qb, k0, nk = UNITS[u]
                    pe.wait_ge(probs_ready, NU * j + (u + 1))
                    if u >= 2 or not first:
                        pe.wait_ge(turned_copied, NU * j + (u - 1))
                    for k in range(nk):
                        ins = pe.transpose(banks[:, 4 + u % 2, bass.ts(k, P)], probs[u % 2][:, bass.ts(k, P)], ident[:, :])
                    ins.then_inc(turned, 1)

                def mix(u):
                    kind, a, qb, k0, nk = UNITS[u]
                    hs = slice(a * HD, (a + 1) * HD)
                    pe.wait_ge(turned_copied, NU * j + (u + 1))
                    o = banks[hs, 6 + (kind == "swa"), bass.ts(qb, P)]
                    val = vv if kind == "fox" else swa_v
                    for k in range(nk):
                        ins = pe.matmul(o, val[:, k0 + k, hs], probs_t[u % 2][:, k, :], start=(k == 0), stop=(k == nk - 1))
                    ins.then_inc(head_mixed, 1)

                for u in range(NU + 2):
                    if u < NU:
                        logits(u)
                    if 1 <= u <= NU:
                        turn(u - 1)
                    if 2 <= u:
                        mix(u - 2)

            pair(0, True)
            with pe.Fori(1, PAIRS) as j:
                pair(j, False)

            def combine(c, it, h_at, l_at, start, stop):
                h, l = hi[c % PART_SLOTS], lo[c % PART_SLOTS]
                for b in range(TB):
                    for n in range(2):
                        o, s = banks[:, 2 * b + n, :], bass.ts(n, 512)
                        pe.matmul(o, h_at(b), h[:, s], start=start, stop=False)
                        pe.matmul(o, h_at(b), l[:, s], start=False, stop=False)
                        ins = pe.matmul(o, l_at(b), h[:, s], start=False, stop=stop)
                ins.then_inc(tile_used, 1)
                return ins

            pe.wait_ge(mix_lo_ready, 2 * PAIRS)
            for r in range(KT):
                pe.wait_ge(lo_ready, S_WOUT + r + 1)
                combine(S_WOUT + r, 0, lambda b: mix_hi[:, r, bass.ts(b, P)], lambda b: mix_lo[:, r, bass.ts(b, P)],
                        r == 0, r == KT - 1)

            for b in range(TB):
                pe.wait_ge(x1_ready, b + 1)
                for k in range(KT):
                    ins = pe.transpose(banks[:, 2 * b + k // 4, bass.ts(k % 4, P)], x1[:, b, bass.ts(k, P)], ident[:, :])
                ins.then_inc(x1_turned, 1)

            pe.wait_ge(x1T_lo_ready, TB)
            pe.wait_ge(keys_loaded, 16)

            def score(l, it):
                pe.wait_ge(qh_ready, 4 * it + (l + 1))
                wait(pe, scores_ready, 4 * it + (l - 1))
                for b in range(TB):
                    ins = pe.matmul(banks[:, 2 + l % 2, bass.ts(b, P)], qh[l % 2][:, bass.ts(b, P)],
                                    keys[:, bass.ds(4 * it + l, 1), :].rearrange("p o n -> p (o n)"),
                                    start=True, stop=True)
                ins.then_inc(scored, 1)

            def query_group(it):
                for l in range(4):
                    wait(pe, qh_ready, 4 * it + (l - 1))
                    features(S_PQ + l, it, l % 2, x1T_hi, x1T_lo)
                    score(l, it)

            query_group(0)
            with pe.Fori(1, LISTS // 4) as it:
                query_group(it)

            def expert_tile(k, it, first=False):
                if first:
                    pe.wait_ge(qh_ready, LISTS)
                else:
                    pe.wait_ge(gelu_ready, 4 * it + (k - 1))
                features(S_U + k, it, k % 2, x1T_hi, x1T_lo)

            for k in range(4):
                expert_tile(k, 0, first=k < 2)
            with pe.Fori(1, A_PRE // 4) as it:
                for k in range(4):
                    expert_tile(k, it)

            pe.wait_ge(gates_ready, 1)
            for m in range(3):
                for b in range(TB):
                    ins = pe.transpose(banks[:, 2 + m, bass.ts(b, P)], sel[:, m, b, :], ident[:, :])
                ins.then_inc(sel_turned, 1)
            pe.wait_ge(selT_ready, 3)

            def scatter(tile, o, first):
                slot = tile % 2
                pe.wait_ge(onehot_ready, 16 * o + (tile + 1))
                for g in range(2):
                    if not first:
                        pe.wait_ge(staged, 32 * o + (2 * tile + g - 1))
                    for k in range(4 * g, 4 * g + 4):
                        r = banks[:, 2 + g, bass.ts(k % 4, NKEY)]
                        pe.matmul(r, onehot[slot][0][:, k, :], onehot[slot][1][:, k, :], start=True, stop=False)
                        ins = pe.matmul(r, onehot[slot][0][:, k, :], onehot[slot][2][:, k, :], start=False, stop=True)
                    ins.then_inc(scattered, 1)

            def two_chunks(o, first):
                for tile in range(2 * TILES_PER_CHUNK):
                    expert_tile(tile % 4, 4 * o + (A_PRE // 4 + tile // 4))
                    scatter(tile, o, first and tile == 0)

            two_chunks(0, True)
            with pe.Fori(1, CHUNKS // 2) as o:
                two_chunks(o, False)
            for it in range((A_PRE + A_MID) // 4, ETILES // 4):
                for k in range(4):
                    expert_tile(k, it)

            pe.wait_ge(gelu_ready, ETILES)
            pe.wait_ge(staged, SEQ // 4)
            pe.wait_ge(zeros_ready, 1)
            for n in range(8):
                pe.matmul(banks[:, n, :], zeros[:, 0:P], zeros[:, :], start=True, stop=False)

            def experts(k, it):
                pe.wait_ge(lo_ready, 4 * it + (S_V + k + 1))
                pe.wait_ge(wgt_lo_ready, 4 * it + (k + 1))
                slot = k % 2
                combine(S_V + k, it, lambda b: wgt_hi[slot][:, bass.ts(b, P)], lambda b: wgt_lo[slot][:, bass.ts(b, P)],
                        False, False)

            with pe.Fori(0, ETILES // 8) as i:
                for k in range(8):
                    experts(k, 2 * i)
            for n in range(8):
                ins = pe.matmul(banks[:, n, :], zeros[:, 0:P], zeros[:, :], start=False, stop=True)
            ins.then_inc(combined, 1)


def kernel(x, ln1_g, ln1_b, w_in, b_f, sink, w_out, ln2_g, ln2_b, w_pq, peer_keys1, peer_keys2, peer_u, peer_v):
    import numpy as np
    import concourse.bacc as bacc
    from concourse.bass_utils import run_bass_kernel_spmd

    def tiles(w):
        n = w.shape[1] // P
        return np.ascontiguousarray(w.reshape(KT, P, n, P).transpose(2, 1, 0, 3)).reshape(n, P, D)

    x, w_in, w_out = np.asarray(x)[0], np.asarray(w_in)[0], np.asarray(w_out)[0]
    fox_q, fox_k, fox_v, w_f, swa_q, swa_k, swa_v = np.split(w_in, [512, 1024, 1536, 1544, 2056, 2184], axis=1)
    order = [h for j in range(PAIRS) for h in (j, PAIRS + j)]
    swa_q = swa_q.reshape(D, HEADS, HD)[:, order].reshape(D, HEADS * HD)
    swa_rows = w_out[512:].reshape(HEADS, HD, D)[order].reshape(HEADS * HD, D)
    fq, fk, fv, sq = tiles(fox_q), tiles(fox_k), tiles(fox_v), tiles(swa_q)
    looped = [t[j] for j in range(PAIRS) for t in (fq, fk, fv, sq)]
    w1 = np.stack([tiles(swa_k)[0], tiles(swa_v)[0], *looped, *w_out[:512].reshape(4, P, D), *swa_rows.reshape(4, P, D)])

    blocked = -2.0 ** 100
    i = np.arange(P)
    mask = np.zeros((P, 4 * P), np.float32)
    mask[:, 3 * P:] = np.where(i[None, :] <= i[:, None], 0.0, blocked)
    key = np.arange(SWA_KEYS)[None, :] - P
    chunks_back = i[:, None] // 64 - key // 64
    seen = (chunks_back >= 0) & (chunks_back <= 1)
    slopes = 2.0 ** -(np.array(order) + 1.0)
    bias = np.where(seen[:, None, :], -slopes[None, :, None] * np.abs(i[:, None] - key)[:, None, :], blocked)
    consts = np.concatenate([mask, bias.reshape(P, -1), np.eye(P), np.tile(i, (P, 1))], axis=1).astype(np.float32)

    keys = np.stack([np.asarray(peer_keys1)[0], np.asarray(peer_keys2)[0]], axis=1).reshape(LISTS, NKEY, P)
    u = np.asarray(peer_u)[0]
    arrays = {
        "x_t": x.T.reshape(KT, P, SEQ).transpose(1, 0, 2),
        "x_rows": x.reshape(TB, P, D).transpose(1, 0, 2),
        "w1": w1,
        "w_ff": w_f.reshape(KT, P, HEADS).transpose(1, 0, 2),
        "b_f": np.asarray(b_f).reshape(HEADS, 1),
        "sinks": np.broadcast_to(np.asarray(sink)[0][order], (P, HEADS)),
        "ln_par": np.broadcast_to(np.stack([np.asarray(a)[0] for a in (ln1_g, ln1_b, ln2_g, ln2_b)]), (P, 4, D)),
        "w_pq": tiles(np.asarray(w_pq)[0]),
        "keys_t": keys.transpose(2, 0, 1),
        "u_t": u.reshape(ETILES, P, KT, P).transpose(0, 3, 2, 1).reshape(ETILES, P, D),
        "v_tab": np.asarray(peer_v)[0].reshape(ETILES, P, D),
        "consts": consts,
    }
    arrays = {n: np.ascontiguousarray(a) for n, a in arrays.items()}
    nc = bacc.Bacc("TRN2", target_bir_lowering=False, num_devices=1)
    args = [nc.dram_tensor(n, a.shape, F32, kind="ExternalInput").ap() for n, a in arrays.items()]
    args.append(nc.dram_tensor("out", (SEQ, D), F32, kind="ExternalOutput").ap())
    build(nc, *args)
    r = run_bass_kernel_spmd(nc, [arrays], core_ids=[0])
    return r.results[0]["out"].reshape(1, SEQ, D)
```

```python
from contextlib import ExitStack

import concourse.bass as bass
from concourse import mybir

F32 = mybir.dt.float32
F32R = mybir.dt.float32r
U32 = mybir.dt.uint32
ALU = mybir.AluOpType
ACT = mybir.ActivationFunctionType
AX_X = mybir.AxisListType.X

P = 128
SEQ = 512
D = 1024
KT = D // P
TB = SEQ // P
HEADS = 8
PAIRS = HEADS // 2
HD = 64
SWA_KEYS = 2 * P
LISTS = 16
PH = 8
TOPK = 16
NKEY = 128
ETILES = 128
EPS = 1e-5
ALPHA = 2.0 ** 0.25
NEG_MAX = -3.0e38

RAW_SLOTS = 4
PART_SLOTS = 2
S_LOOP = 2
S_WOUT = S_LOOP + 4 * PAIRS
S_PQ = S_WOUT + KT
S_U = S_PQ + LISTS
S_V = S_U + ETILES
N_TILES = S_V + ETILES

DENSE = SEQ - P
RANKS = PH * TOPK
ROWS = 8

OCTETS = ETILES // 8
O_IDLE = 2
O_PRE = 8
TOK_PER_TILE = 8
CHUNK = 32
TILES_PER_CHUNK = CHUNK // TOK_PER_TILE
CHUNKS = DENSE // CHUNK
O_MID = CHUNKS // 2
A_PRE = 8 * O_PRE
A_MID = 8 * O_MID
R_PRE = O_PRE - O_IDLE
R_MID = O_MID
R_ALL = RANKS // ROWS
AHEAD = 4
ROUTE_STEPS = 1 + 5 + 2 + 5 + 2 + 2 + 6
TILES_PER_CHUNK = CHUNK // TOK_PER_TILE


def build(nc, x_t, x_rows, w1, w_ff, b_f, sinks, ln_par, w_pq, keys_t, u_t, u_rows, v_tab, consts, out):
    g_dram = nc.dram_tensor("g_scratch", (CHUNKS, P, ETILES, CHUNK), F32, kind="Internal").ap()
    a_dram = nc.dram_tensor("gelu_scratch", (ETILES // 4, P, 4, DENSE), F32, kind="Internal").ap()
    c_dram = nc.dram_tensor("decay_scratch", (4, HEADS, SEQ), F32R, kind="Internal").ap()

    ctx = ExitStack()
    with ctx:
        def sb(name, shape, dt=F32, stack=ctx):
            return stack.enter_context(nc.sbuf_tensor(name, shape, dt))

        def sem(name):
            return ctx.enter_context(nc.semaphore(name))

        raw = sb("raw", [P, RAW_SLOTS, D])
        hi = [sb(f"hi{i}", [P, D], F32R) for i in range(PART_SLOTS)]
        lo = [sb(f"lo{i}", [P, D], F32R) for i in range(PART_SLOTS)]
        x1 = sb("x1", [P, TB, D])
        ident = sb("ident", [P, P])
        iota = sb("iota", [P, NKEY])
        stats = sb("stats", [P, TB, 2, 6])
        moments = sb("moments", [P, TB, 2])
        rstd = sb("rstd", [P, TB, 6])

        att = ExitStack()
        xbuf = sb("xbuf", [P, KT * SEQ], F32, att)
        xT = xbuf[:, :].rearrange("p (k t) -> p k t", k=KT)
        xR = xbuf[:, :].rearrange("p (b d) -> p b d", b=TB)
        xT_hi = sb("xT_hi", [P, KT, SEQ], F32R, att)
        xT_lo = sb("xT_lo", [P, KT, SEQ], F32R, att)
        ff_w = sb("ff_w", [P, KT, HEADS], F32, att)
        ff_b = sb("ff_b", [HEADS, 1], F32, att)
        sink = sb("sink", [P, HEADS], F32, att)
        neg_sink = sb("neg_sink", [P, HEADS], F32, att)
        cst = sb("cst", [P, 4 * P + HEADS * SWA_KEYS], F32, att)
        ident_r = sb("ident_r", [P, P], F32R, att)
        mask_r = sb("mask_r", [P, 4 * P], F32R, att)
        bias_r = sb("bias_r", [P, HEADS, SWA_KEYS], F32R, att)
        ff = [sb(f"ff{i}", [HEADS, SEQ], F32, att) for i in range(5)]
        decay_r = sb("decay_r", [HEADS, 4, SEQ], F32R, att)
        decay_q = sb("decay_q", [4, 2, SEQ], F32R, att)
        decay_k = sb("decay_k", [4, 2, SEQ], F32R, att)
        qT = sb("qT", [P, SEQ], F32, att)
        kT = sb("kT", [P, SEQ], F32, att)
        vv = sb("vv", [P, TB, P], F32, att)
        swa_q = sb("swa_q", [P, SEQ], F32, att)
        swa_k = sb("swa_k", [P, SEQ], F32, att)
        swa_v = sb("swa_v", [P, TB, P], F32, att)
        probs = [sb(f"probs{i}", [P, SEQ], F32, att) for i in range(3)]
        probs_t = [sb(f"probs_t{i}", [P, 4, P], F32, att) for i in range(2)]
        row = [sb(f"row{i}", [P, 8], F32, att) for i in range(3)]
        mix_hi = sb("mix_hi", [P, KT, SEQ], F32R, att)
        mix_lo = sb("mix_lo", [P, KT, SEQ], F32R, att)
        ln1_gb = sb("ln1_gb", [P, 2, D], F32, att)
        att.close()

        x1T_hi = sb("x1T_hi", [P, KT, SEQ], F32R)
        x1T_lo = sb("x1T_lo", [P, KT, SEQ], F32R)
        sel = sb("sel", [P, 3, TB, P])
        selT = sb("selT", [P, 3, DENSE])
        gateT_hi = sb("gateT_hi", [P, DENSE])
        gateT_lo = sb("gateT_lo", [P, DENSE])
        gate_r = sb("gate_r", [P, DENSE], F32R)
        gelu = [sb(f"gelu{i}", [P, DENSE]) for i in range(2)]
        rows = sb("rows", [P, ROWS, D])
        expert = sb("expert", [P, RANKS], U32)
        expert_at = [sb(f"expert_at{i}", [P, 1], U32) for i in range(ROWS)]
        dots8 = sb("dots8", [P, ROWS])
        dots = sb("dots", [P, RANKS])
        dots_gelu = sb("dots_gelu", [P, RANKS])
        row_weight = sb("row_weight", [P, RANKS])
        route = ExitStack()
        keys = sb("keys", [P, LISTS, NKEY], F32, route)
        qh = [sb(f"qh{i}", [P, SEQ], F32, route) for i in range(2)]
        scores = sb("scores", [P, TB, LISTS, NKEY], F32, route)
        work = sb("work", [P, LISTS, NKEY], F32, route)
        best = sb("best", [P, LISTS, TOPK], F32, route)
        best_i = sb("best_i", [P, LISTS, TOPK], U32, route)
        best_f = sb("best_f", [P, LISTS, TOPK], F32, route)
        cand = sb("cand", [P, PH, TOPK * TOPK], F32, route)
        match = cand
        prod = work
        top = sb("top", [P, PH, TOPK], F32, route)
        top_i = sb("top_i", [P, PH, TOPK], U32, route)
        pos_u = sb("pos_u", [P, 2, P], U32, route)
        pos_f = sb("pos_f", [P, 2, P], F32, route)
        gsum = sb("gsum", [P, 2, TB * PH], F32, route)
        route.close()
        scat = ExitStack()
        onehot = [[sb(f"onehot{i}_{j}", [P, TOK_PER_TILE, NKEY], F32R, scat) for j in range(3)] for i in range(2)]
        is_i1 = sb("is_i1", [P, TOK_PER_TILE, NKEY], F32, scat)
        stage = [sb(f"stage{i}", [P, ETILES, CHUNK], F32, scat) for i in range(2)]
        scat.close()
        comb = ExitStack()
        ga = [sb(f"ga{i}", [P, 4, DENSE], F32, comb) for i in range(2)]
        gg = [sb(f"gg{i}", [P, CHUNKS, 4, CHUNK], F32, comb) for i in range(2)]
        wgt = [sb(f"wgt{i}", [P, DENSE], F32, comb) for i in range(2)]
        wgt_hi = [sb(f"wgt_hi{i}", [P, DENSE], F32R, comb) for i in range(2)]
        wgt_lo = [sb(f"wgt_lo{i}", [P, DENSE], F32R, comb) for i in range(2)]
        ln2_gb = sb("ln2_gb", [P, 2, D], F32, comb)
        zeros = sb("zeros", [P, SEQ], F32R, comb)
        comb.close()

        banks = ctx.enter_context(nc.psum_tensor("banks", [P, 8, 512], F32))

        raw_loaded = [sem(f"raw_loaded{i}") for i in range(RAW_SLOTS)]
        hi_ready = sem("hi_ready")
        lo_ready = sem("lo_ready")
        tile_used = sem("tile_used")
        xT_loaded = sem("xT_loaded")
        small_loaded = sem("small_loaded")
        xR_loaded = sem("xR_loaded")
        ln_loaded = sem("ln_loaded")
        xT_split = sem("xT_split")
        consts_ready = sem("consts_ready")
        ff_ready = sem("ff_ready")
        ff_step = sem("ff_step")
        decay_ready = sem("decay_ready")
        decay_stored = sem("decay_stored")
        decay_loaded = sem("decay_loaded")
        proj_copied = sem("proj_copied")
        logits_ready = sem("logits_ready")
        max_step = sem("max_step")
        max_ready = sem("max_ready")
        exp_ready = sem("exp_ready")
        norm_step = sem("norm_step")
        probs_ready = sem("probs_ready")
        turned = sem("turned")
        turned_copied = sem("turned_copied")
        head_mixed = sem("head_mixed")
        mix_hi_ready = sem("mix_hi_ready")
        mix_lo_ready = sem("mix_lo_ready")
        ln_step = sem("ln_step")
        sqrt_ready = sem("sqrt_ready")
        norm_chain = sem("norm_chain")
        x1_ready = sem("x1_ready")
        x1_turned = sem("x1_turned")
        x1T_hi_ready = sem("x1T_hi_ready")
        x1T_lo_ready = sem("x1T_lo_ready")
        keys_loaded = sem("keys_loaded")
        qh_ready = sem("qh_ready")
        scored = sem("scored")
        scores_ready = sem("scores_ready")
        route_step = sem("route_step")
        route_tick = sem("route_tick")
        gate_exp = sem("gate_exp")
        gate_step = sem("gate_step")
        gates_ready = sem("gates_ready")
        sel_turned = sem("sel_turned")
        selT_ready = sem("selT_ready")
        gelu_ready = sem("gelu_ready")
        expert_ready = sem("expert_ready")
        expert_at_ready = sem("expert_at_ready")
        gathered = [sem(f"gathered{i}") for i in range(ROWS)]
        row_used = sem("row_used")
        dots8_free = sem("dots8_free")
        dots_gelu_ready = sem("dots_gelu_ready")
        residual_ready = sem("residual_ready")
        row_weight_ready = sem("row_weight_ready")
        gelu_stored = [sem(f"gelu_stored{i}") for i in range(2)]
        onehot_ready = sem("onehot_ready")
        is_i1_ready = sem("is_i1_ready")
        scattered = sem("scattered")
        staged = sem("staged")
        g_stored = [sem(f"g_stored{i}") for i in range(2)]
        comb_loaded = [sem(f"comb_loaded{i}") for i in range(2)]
        wgt_ready = sem("wgt_ready")
        wgt_hi_ready = sem("wgt_hi_ready")
        wgt_lo_ready = sem("wgt_lo_ready")
        zeros_ready = sem("zeros_ready")
        combined = sem("combined")
        y_ready = sem("y_ready")
        out_stored = sem("out_stored")

        def wait(eng, s, value):
            if not (isinstance(value, int) and value <= 0):
                eng.wait_ge(s, value)


        def load_tile(eng, c, it, src):
            wait(eng, lo_ready, 4 * it + (c - RAW_SLOTS + 1))
            eng.dma_start(raw[:, c % RAW_SLOTS, :], src).then_inc(raw_loaded[c % RAW_SLOTS], 16)

        def split_hi(act, c, it):
            wait(act, raw_loaded[c % RAW_SLOTS], 16 * it + 16 * (c // RAW_SLOTS + 1))
            wait(act, tile_used, 4 * it + (c - PART_SLOTS + 1))
            act.activation(hi[c % PART_SLOTS][:, :], raw[:, c % RAW_SLOTS, :], ACT.Copy).then_inc(hi_ready, 1)

        def split_lo(eng, c, it):
            wait(eng, hi_ready, 4 * it + (c + 1))
            eng.tensor_tensor(lo[c % PART_SLOTS][:, :], raw[:, c % RAW_SLOTS, :],
                              hi[c % PART_SLOTS][:, :].bitcast(F32), ALU.subtract).then_inc(lo_ready, 1)

        def units():
            for a in range(2):
                for qb in range(TB):
                    yield "fox", a, qb, 0, qb + 1
            for a in range(2):
                for qb in range(TB):
                    yield "swa", a, qb, max(qb - 1, 0), min(qb, 1) + 1

        UNITS = list(units())
        NU = len(UNITS)
        SWA_UNITS = NU // 2

        TURN_LAG, MIX_LAG = 2, 3
        STEPS = NU + MIX_LAG
        PROJ_AT = {8: (0, 3), 11: (1, 3), 14: (2, 3), 17: (3, 2)}

        def count_swa(u):
            return sum(1 for k in UNITS[:u] if k[0] == "swa")

        block = ctx.enter_context(nc.Block())

        @block.sync
        def _(sp):
            sp.dma_start(xT, x_t).then_inc(xT_loaded, 16)
            for c in range(S_LOOP):
                load_tile(sp, c, 0, w1[c])
            sp.dma_start(cst[:, :], consts[:, 0:4 * P + HEADS * SWA_KEYS]).then_inc(small_loaded, 16)
            sp.dma_start(ident[:, :], consts[:, 4 * P + HEADS * SWA_KEYS:5 * P + HEADS * SWA_KEYS]).then_inc(small_loaded, 16)
            sp.dma_start(iota[:, :], consts[:, 5 * P + HEADS * SWA_KEYS:]).then_inc(small_loaded, 16)
            sp.dma_start(ff_w[:, :, :], w_ff).then_inc(small_loaded, 16)
            sp.dma_start(ff_b[:, :], b_f).then_inc(small_loaded, 16)
            sp.dma_start(sink[:, :], sinks).then_inc(small_loaded, 16)
            sp.dma_start(ln1_gb[:, :, :], ln_par[:, 0:2, :]).then_inc(ln_loaded, 16)
            for c in range(S_LOOP, S_LOOP + 4):
                load_tile(sp, c, 0, w1[c])
            with sp.Fori(1, PAIRS) as j:
                for k in range(4):
                    load_tile(sp, S_LOOP + k, j, w1[4 * j + (S_LOOP + k)])
            sp.wait_ge(xT_split, 2)
            sp.wait_ge(ff_ready, 1)
            sp.dma_start(xR, x_rows).then_inc(xR_loaded, 16)
            for c in range(S_WOUT, S_PQ):
                load_tile(sp, c, 0, w1[c])
            for c in range(S_PQ, S_PQ + 4):
                load_tile(sp, c, 0, w_pq[c - S_PQ])
            sp.wait_ge(x1T_lo_ready, TB)
            sp.dma_start(keys[:, :, :], keys_t).then_inc(keys_loaded, 16)
            with sp.Fori(1, LISTS // 4) as i:
                for k in range(4):
                    load_tile(sp, S_PQ + k, i, w_pq[4 * i + k])

            def store_gelu(slot, n_it, k, value):
                sp.wait_ge(gelu_ready, value)
                sp.dma_start(a_dram[n_it, :, k, :], gelu[slot][:, :]).then_inc(gelu_stored[slot], 16)

            for k in range(4):
                load_tile(sp, S_U + k, 0, u_t[k])

            def tiles_and_stores(it):
                for k in range(4):
                    load_tile(sp, S_U + 4 + k, it, u_t[4 * it + (4 + k)])
                    store_gelu(k % 2, it, k, 4 * it + (k + 1))

            with sp.Fori(0, A_PRE // 4) as it:
                tiles_and_stores(it)
            with sp.Fori(0, O_MID) as o:
                for half in range(2):
                    tiles_and_stores(2 * o + (A_PRE // 4 + half))
                    sp.wait_ge(staged, 4 * TILES_PER_CHUNK * o + 2 * TILES_PER_CHUNK * (half + 1))
                    sp.dma_start(g_dram[2 * o + half], stage[half][:, :, :]).then_inc(g_stored[half], 16)
            for it in range((A_PRE + A_MID) // 4, ETILES // 4 - 1):
                tiles_and_stores(it)
            for k in range(4):
                load_tile(sp, S_V + k, 0, v_tab[k])
                store_gelu(k % 2, ETILES // 4 - 1, k, ETILES - 4 + k + 1)
            for half in range(2):
                sp.wait_ge(gelu_stored[half], 16 * ETILES // 2)
                sp.wait_ge(g_stored[half], 16 * CHUNKS // 2)

            def load_group(g, slot):
                sp.dma_start(ga[slot][:, :, :], a_dram[g]).then_inc(comb_loaded[slot], 16)
                sp.dma_start(gg[slot][:, :, :, :],
                             g_dram[:, :, bass.ds(4 * g, 4), :].rearrange("c p n t -> p c n t")
                             ).then_inc(comb_loaded[slot], 16)

            load_group(0, 0)
            load_group(1, 1)
            sp.dma_start(ln2_gb[:, :, :], ln_par[:, 2:4, :]).then_inc(ln_loaded, 16)
            for k in range(4):
                load_tile(sp, S_V + 4 + k, 0, v_tab[4 + k])
            with sp.Fori(1, ETILES // 8) as i:
                for slot in range(2):
                    sp.wait_ge(wgt_ready, 8 * i + (4 * slot - 4))
                    load_group(2 * i + slot, slot)
                    for k in range(4):
                        load_tile(sp, S_V + 4 * slot + k, 2 * i, v_tab[8 * i + (4 * slot + k)])
            for b in range(TB):
                sp.wait_ge(y_ready, b + 1)
                sp.dma_start(out[bass.ts(b, P), :], x1[:, b, :]).then_inc(out_stored, 16)
            sp.wait_ge(out_stored, 16 * TB)

        @block.gpsimd
        def _(pool):
            pool.memset(decay_q[:, :, :].bitcast(F32), 1.0).then_inc(decay_ready, 1)
            pool.memset(decay_k[:, :, :].bitcast(F32), 1.0).then_inc(decay_ready, 1)
            for c in range(S_LOOP):
                split_lo(pool, c, 0)
            pool.wait_ge(decay_ready, 6)
            pool.dma_start(c_dram.rearrange("r h t -> h r t"), decay_r[:, :, :]).then_inc(decay_stored, 16)
            pool.wait_ge(decay_stored, 16)

            def load_decay(j):
                pool.dma_start(decay_q[2:4, :, :], c_dram[0:2, bass.ds(2 * j, 2), :]).then_inc(decay_loaded, 16)
                pool.dma_start(decay_k[0:2, :, :], c_dram[2:4, bass.ds(2 * j, 2), :]).then_inc(decay_loaded, 16)

            load_decay(0)
            for k in range(6):
                split_lo(pool, S_LOOP + k, 0)
            with pool.Fori(0, PAIRS - 1) as j:
                pool.wait_ge(logits_ready, NU * j + SWA_UNITS)
                load_decay(j + 1)
                for k in range(6, 10):
                    split_lo(pool, S_LOOP + k, j)
            for c in range(S_WOUT + 2, S_PQ):
                split_lo(pool, c, 0)
            with pool.Fori(0, (S_U - S_PQ) // 8 + O_IDLE) as o:
                for k in range(8):
                    split_lo(pool, S_PQ + k, 2 * o)

            v_rows = v_tab.rearrange("n p d -> (n p) d")

            def gather(table, ks, r, tile=None):
                first = 0 if table is u_rows else RANKS
                for k in ks:
                    wait(pool, row_used, ROWS * r + (k + 1 - ROWS))
                    pool.tensor_copy(expert_at[k % ROWS][:, :],
                                     expert[:, bass.ds(ROWS * r + (k - first), 1)]).then_inc(expert_at_ready, 1)
                pool.wait_ge(expert_at_ready, ROWS * r + (ks[-1] + 1))
                split_lo(pool, *tile)
                for k in ks:
                    at = bass.IndirectOffsetOnAxis(ap=expert_at[k % ROWS][:, :], axis=0)
                    pool.indirect_dma_start(rows[:, k % ROWS, :], None, table, at).then_inc(gathered[k % ROWS], 16)

            pool.wait_ge(expert_ready, 1)
            gather(u_rows, range(AHEAD + 1), 0, (S_U + 8 * O_IDLE, 0))
            for k in range(1, 8):
                gather(u_rows, [k + AHEAD], 0, (S_U + 8 * O_IDLE + k, 0))
            with pool.Fori(1, R_PRE + R_MID) as r:
                for k in range(8):
                    gather(u_rows, [k + AHEAD], r, (S_U + 8 * O_IDLE + k, 2 * r))
            for k in range(A_PRE + A_MID, ETILES):
                rank = ROWS * (R_PRE + R_MID) + AHEAD + 2 * (k - A_PRE - A_MID)
                gather(u_rows if rank < RANKS else v_rows, [rank, rank + 1], 0, (S_U + k, 0))
            with pool.Fori(0, OCTETS - 1) as o:
                for k in range(8):
                    gather(v_rows, [k + AHEAD + RANKS], o, (S_V + k, 2 * o))
            for k in range(8):
                tile = (N_TILES - 8 + k, 0)
                if k + AHEAD < 8:
                    gather(v_rows, [k + AHEAD + 2 * RANKS - 8], 0, tile)
                else:
                    split_lo(pool, *tile)

        @block.scalar
        def _(act):
            act.wait_ge(xT_loaded, 16)
            act.activation(xT_hi[:, :, :], xT, ACT.Copy).then_inc(xT_split, 1)
            for c in range(S_LOOP):
                split_hi(act, c, 0)
            act.wait_ge(small_loaded, 96)
            act.activation(mask_r[:, :], cst[:, 0:4 * P], ACT.Copy).then_inc(consts_ready, 1)
            act.activation(bias_r[:, :, :], cst[:, 4 * P:].rearrange("p (h k) -> p h k", h=HEADS),
                           ACT.Copy).then_inc(consts_ready, 1)
            act.activation(ident_r[:, :], ident[:, :], ACT.Copy).then_inc(consts_ready, 1)
            act.wait_ge(ff_ready, 1)
            act.activation(ff[0][:, :], banks[0:HEADS, 2, :], ACT.Identity, bias=ff_b[:, :]).then_inc(ff_step, 1)
            act.wait_ge(ff_step, 1)
            act.activation(ff[1][:, :], ff[0][:, :], ACT.Abs).then_inc(ff_step, 1)
            act.wait_ge(ff_step, 2)
            act.activation(ff[2][:, :], ff[1][:, :], ACT.Exp, scale=-1.0).then_inc(ff_step, 1)
            act.wait_ge(ff_step, 3)
            act.activation(ff[3][:, :], ff[2][:, :], ACT.Ln, bias=1.0).then_inc(ff_step, 1)

            def copy_proj(value, dst, bank, scale=1.0):
                act.wait_ge(tile_used, value)
                act.activation(dst, banks[:, bank, :], ACT.Copy, scale=scale).then_inc(proj_copied, 1)

            copy_proj(1, swa_k[:, :], 0)
            copy_proj(2, swa_v[:, :, :].rearrange("p b d -> p (b d)"), 1)
            for k in range(2):
                split_hi(act, S_LOOP + k, 0)

            PROJ_OUT = ((qT[:, :], HD ** -0.5), (kT[:, :], 1.0), (vv[:, :, :].rearrange("p b d -> p (b d)"), 1.0),
                        (swa_q[:, :], HD ** -0.5))

            def projected(k, j):
                copy_proj(4 * j + (S_LOOP + k + 1), PROJ_OUT[k][0], k % 2, PROJ_OUT[k][1])
                split_hi(act, S_LOOP + k + 2, j)

            for k in range(4):
                projected(k, 0)

            def pair(j, last):
                def exponentials(u):
                    kind, a, qb, k0, nk = UNITS[u]
                    act.wait_ge(max_ready, NU * j + (u + 1))
                    r = row[u % 3]
                    ins = act.activation(probs[u % 3][:, 0:nk * P], banks[:, 2 + u % 2, 0:nk * P], ACT.Exp,
                                         bias=r[:, 1:2], accum_out=r[:, 2:3])
                    if kind == "swa":
                        ins = act.activation(r[:, 3:4], sink[:, bass.ds(2 * j + a, 1)], ACT.Exp, bias=r[:, 1:2])
                    ins.then_inc(exp_ready, 1)

                def copy_turned(u):
                    kind, a, qb, k0, nk = UNITS[u]
                    act.wait_ge(turned, NU * j + (u + 1))
                    if u >= 2:
                        act.wait_ge(head_mixed, NU * j + (u - 1))
                    act.activation(probs_t[u % 2][:, 0:nk, :],
                                   banks[:, 4 + u % 2, 0:nk * P].rearrange("p (k q) -> p k q", k=nk),
                                   ACT.Copy).then_inc(turned_copied, 1)

                def outputs_hi(g):
                    act.wait_ge(head_mixed, NU * j + SWA_UNITS * (g + 1))
                    act.activation(mix_hi[:, bass.ds(j + PAIRS * g, 1), :].rearrange("p o t -> p (o t)"),
                                   banks[:, 6 + g, :], ACT.Copy).then_inc(mix_hi_ready, 1)

                for step in range(STEPS + 1):
                    if step < NU:
                        exponentials(step)
                    if 0 <= step - TURN_LAG < NU:
                        copy_turned(step - TURN_LAG)
                    if step == SWA_UNITS + MIX_LAG:
                        outputs_hi(0)
                    for first, (k, n) in PROJ_AT.items():
                        if not last and step == first + n:
                            projected(k, j + 1)
                outputs_hi(1)

            with act.Fori(0, PAIRS - 1) as j:
                pair(j, False)
            pair(PAIRS - 1, True)
            for c in range(S_WOUT + 2, S_PQ + 1 + 1):
                split_hi(act, c, 0)

            for b in range(TB):
                act.wait_ge(ln_step, 3 * (b + 1))
                act.activation(rstd[:, b, 1:2], rstd[:, b, 0:1], ACT.Sqrt).then_inc(sqrt_ready, 1)
            for b in range(TB):
                act.wait_ge(x1_turned, b + 1)
                act.activation(x1T_hi[:, :, bass.ts(b, P)],
                               banks[:, 2 * b:2 * b + 2, :].rearrange("p h (k t) -> p (h k) t", t=P),
                               ACT.Copy).then_inc(x1T_hi_ready, 1)

            def copy_query(l, it):
                act.wait_ge(tile_used, 4 * it + (S_PQ + l + 1))
                wait(act, scored, 4 * it + (l - 1))
                act.activation(qh[l % 2][:, :], banks[:, l % 2, :], ACT.Copy).then_inc(qh_ready, 1)

            def copy_scores(l, it):
                act.wait_ge(scored, 4 * it + (l + 1))
                act.activation(scores[:, :, bass.ds(4 * it + l, 1), :].rearrange("p b o n -> p b (o n)"),
                               banks[:, 2 + l % 2, :].rearrange("p (b n) -> p b n", b=TB),
                               ACT.Copy).then_inc(scores_ready, 1)

            def query_group(it):
                for l in range(4):
                    copy_query(l, it)
                    split_hi(act, S_PQ + 2 + l, it)
                    copy_scores(l, it)

            query_group(0)
            with act.Fori(1, LISTS // 4) as it:
                query_group(it)

            def gelu_tile(k, it, first=False):
                act.wait_ge(tile_used, 4 * it + (S_U + k + 1))
                if not first:
                    act.wait_ge(gelu_stored[k % 2], 32 * it + 16 * (k // 2))
                act.activation(gelu[k % 2][:, :], banks[:, k % 2, 0:DENSE], ACT.Gelu).then_inc(gelu_ready, 1)
                split_hi(act, S_U + 2 + k, it)

            for k in range(4):
                gelu_tile(k, 0, first=k < 2)
            with act.Fori(1, A_PRE // 4) as it:
                for k in range(4):
                    gelu_tile(k, it)

            act.wait_ge(route_step, ROUTE_STEPS * TB)
            act.activation(sel[:, 2, :, :], sel[:, 2, :, :], ACT.Exp).then_inc(gate_exp, 1)
            for m in range(3):
                act.wait_ge(sel_turned, m + 1)
                act.activation(selT[:, m, :], banks[:, 2 + m, 0:DENSE], ACT.Copy).then_inc(selT_ready, 1)

            def stage_gates(chunk_half, o, tile, first):
                for g in range(2):
                    n = 2 * tile + g
                    act.wait_ge(scattered, 4 * TILES_PER_CHUNK * o + (2 * TILES_PER_CHUNK * chunk_half + n + 1))
                    if tile == 0 and g == 0 and not first:
                        act.wait_ge(g_stored[chunk_half], 16 * o)
                    t0 = tile * TOK_PER_TILE + 4 * g
                    act.activation(stage[chunk_half][:, :, t0:t0 + 4].rearrange("p n t -> p t n"),
                                   banks[:, 2 + g, :].rearrange("p (t n) -> p t n", t=4),
                                   ACT.Copy).then_inc(staged, 1)

            def two_chunks(o, first):
                for half in range(2):
                    for tile in range(TILES_PER_CHUNK):
                        gelu_tile(tile, 2 * o + (A_PRE // 4 + half))
                        stage_gates(half, o, tile, first)

            two_chunks(0, True)
            with act.Fori(1, O_MID) as o:
                two_chunks(o, False)
            for it in range((A_PRE + A_MID) // 4, ETILES // 4):
                for k in range(4):
                    gelu_tile(k, it)
            act.wait_ge(dots8_free, R_ALL + 1)
            act.activation(dots_gelu[:, :], dots[:, :], ACT.Gelu).then_inc(dots_gelu_ready, 1)

            def weight_hi(k, it, first=False):
                act.wait_ge(wgt_ready, 4 * it + (k + 1))
                if not first:
                    act.wait_ge(tile_used, 4 * it + (S_V + k - 1))
                act.activation(wgt_hi[k % 2][:, :], wgt[k % 2][:, :], ACT.Copy).then_inc(wgt_hi_ready, 1)

            weight_hi(0, 0, True)
            weight_hi(1, 0, True)
            with act.Fori(0, ETILES // 8 - 1) as i:
                for k in range(8):
                    split_hi(act, S_V + 2 + k, 2 * i)
                    weight_hi(2 + k, 2 * i)
            for k in range(6):
                split_hi(act, N_TILES - 6 + k, 0)
                weight_hi(ETILES - 6 + k, 0)
            for b in range(TB):
                act.wait_ge(ln_step, 3 * (TB + b + 1))
                act.activation(rstd[:, b, 1:2], rstd[:, b, 0:1], ACT.Sqrt).then_inc(sqrt_ready, 1)

        @block.vector
        def _(dve):
            dve.wait_ge(xT_split, 1)
            dve.tensor_tensor(xT_lo[:, :, :], xT, xT_hi[:, :, :].bitcast(F32), ALU.subtract).then_inc(xT_split, 1)
            dve.wait_ge(small_loaded, 96)
            dve.tensor_scalar(neg_sink[:, :], sink[:, :], -1.0, None, ALU.mult).then_inc(consts_ready, 1)
            dve.memset(ff[4][:, :], 1.0).then_inc(max_step, 1)
            dve.wait_ge(ff_step, 4)
            dve.scalar_tensor_tensor(ff[1][:, :], ff[0][:, :], 0.0, ff[3][:, :], ALU.min, ALU.subtract).then_inc(ff_step, 1)
            dve.wait_ge(ff_step, 5)
            dve.wait_ge(max_step, 1)
            dve.tensor_tensor_scan(ff[2][:, :], ff[4][:, :], ff[1][:, :], 0.0, ALU.mult, ALU.add).then_inc(ff_step, 1)
            dve.wait_ge(ff_step, 6)
            dve.tensor_copy(decay_r[:, 0, :], ff[2][:, :]).then_inc(decay_ready, 1)
            dve.wait_ge(decay_ready, 3)
            dve.tensor_tensor(decay_r[:, 1, :], ff[2][:, :], decay_r[:, 0, :].bitcast(F32), ALU.subtract).then_inc(decay_ready, 1)
            dve.tensor_scalar(decay_r[:, 2, :], decay_r[:, 0, :].bitcast(F32), -1.0, None, ALU.mult).then_inc(decay_ready, 1)
            dve.wait_ge(decay_ready, 4)
            dve.tensor_scalar(decay_r[:, 3, :], decay_r[:, 1, :].bitcast(F32), -1.0, None, ALU.mult).then_inc(decay_ready, 1)

            def pair(j):
                def maximum(u):
                    kind, a, qb, k0, nk = UNITS[u]
                    r = row[u % 3]
                    dve.wait_ge(logits_ready, NU * j + (u + 1))
                    src = banks[:, 2 + u % 2, 0:nk * P]
                    if kind == "fox":
                        dve.tensor_reduce(r[:, 1:2], src, AX_X, ALU.max, negate=True).then_inc(max_ready, 1)
                    else:
                        dve.tensor_reduce(r[:, 0:1], src, AX_X, ALU.max, negate=True).then_inc(max_step, 1)
                        dve.wait_ge(max_step, SWA_UNITS * j + (count_swa(u) + 2))
                        dve.tensor_tensor(r[:, 1:2], r[:, 0:1], neg_sink[:, bass.ds(2 * j + a, 1)],
                                          ALU.min).then_inc(max_ready, 1)

                def normalise(u):
                    kind, a, qb, k0, nk = UNITS[u]
                    r = row[u % 3]
                    dve.wait_ge(exp_ready, NU * j + (u + 1))
                    steps = (NU + SWA_UNITS) * j + (u + count_swa(u))
                    if kind == "fox":
                        dve.reciprocal(r[:, 4:5], r[:, 2:3]).then_inc(norm_step, 1)
                        dve.wait_ge(norm_step, steps + 1)
                    else:
                        dve.tensor_tensor(r[:, 5:6], r[:, 2:3], r[:, 3:4], ALU.add).then_inc(norm_step, 1)
                        dve.wait_ge(norm_step, steps + 1)
                        dve.reciprocal(r[:, 4:5], r[:, 5:6]).then_inc(norm_step, 1)
                        dve.wait_ge(norm_step, steps + 2)
                    dve.tensor_scalar(probs[u % 3][:, 0:nk * P], probs[u % 3][:, 0:nk * P], r[:, 4:5], None,
                                      ALU.mult).then_inc(probs_ready, 1)

                def outputs_lo(g):
                    dve.wait_ge(mix_hi_ready, 2 * j + (g + 1))
                    s = bass.ds(j + PAIRS * g, 1)
                    dve.tensor_tensor(mix_lo[:, s, :].rearrange("p o t -> p (o t)"), banks[:, 6 + g, :],
                                      mix_hi[:, s, :].rearrange("p o t -> p (o t)").bitcast(F32),
                                      ALU.subtract).then_inc(mix_lo_ready, 1)

                for step in range(STEPS):
                    if 1 <= step <= NU:
                        normalise(step - 1)
                    if step < NU:
                        maximum(step)
                    if step == SWA_UNITS + MIX_LAG + 1:
                        outputs_lo(0)
                outputs_lo(1)

            with dve.Fori(0, PAIRS) as j:
                pair(j)

            def layer_norm(b, rows, n, done):
                base = 3 * n
                for h in range(2):
                    ins = dve.bn_stats(stats[:, b, h, :], rows[:, bass.ts(h, 512)])
                ins.then_inc(ln_step, 1)
                dve.wait_ge(ln_step, base + 1)
                dve.bn_aggr(moments[:, b, :], stats[:, b, :, :]).then_inc(ln_step, 1)
                dve.wait_ge(ln_step, base + 2)
                dve.tensor_scalar(rstd[:, b, 0:1], moments[:, b, 1:2], EPS, None, ALU.add).then_inc(ln_step, 1)

            ln_chain = [0]

            def chained(ins):
                ins.then_inc(norm_chain, 1)
                ln_chain[0] += 1
                dve.wait_ge(norm_chain, ln_chain[0])

            def finish_norm(b, rows, n, gb, done):
                dve.wait_ge(sqrt_ready, n + 1)
                v, s, r0, t, r1 = (rstd[:, b, i:i + 1] for i in range(5))
                chained(dve.reciprocal(r0, s))
                chained(dve.scalar_tensor_tensor(t, r0, v, r0, ALU.mult, ALU.mult))
                chained(dve.tensor_scalar(t, t, -0.5, 1.5, ALU.mult, ALU.add))
                chained(dve.tensor_tensor(r1, r0, t, ALU.mult))
                chained(dve.tensor_scalar(rows, rows, moments[:, b, 0:1], r1, ALU.subtract, ALU.mult))
                chained(dve.tensor_tensor(rows, rows, gb[:, 0, :], ALU.mult))
                dve.tensor_tensor(rows, rows, gb[:, 1, :], ALU.add).then_inc(done, 1)

            dve.wait_ge(xR_loaded, 16)
            dve.wait_ge(ln_loaded, 16)
            dve.wait_ge(tile_used, S_PQ)
            for b in range(TB):
                chained(dve.scalar_tensor_tensor(x1[:, b, :], xR[:, b, :], ALPHA,
                                                 banks[:, 2 * b:2 * b + 2, :].rearrange("p h n -> p (h n)"),
                                                 ALU.mult, ALU.add))
                layer_norm(b, x1[:, b, :], b, None)
            for b in range(TB):
                finish_norm(b, x1[:, b, :], b, ln1_gb, x1_ready)
            for b in range(TB):
                dve.wait_ge(x1T_hi_ready, b + 1)
                dve.tensor_tensor(x1T_lo[:, :, bass.ts(b, P)],
                                  banks[:, 2 * b:2 * b + 2, :].rearrange("p h (k t) -> p (h k) t", t=P),
                                  x1T_hi[:, :, bass.ts(b, P)].bitcast(F32), ALU.subtract).then_inc(x1T_lo_ready, 1)

            def dot(k, r):
                dve.wait_ge(gathered[k], 16 * r + 16)
                if k == 0:
                    dve.wait_ge(dots8_free, r + 1)
                dve.tensor_tensor_reduce(rows[:, k, :], rows[:, k, :], x1[:, 0, :], 1.0, 0.0, ALU.mult, ALU.add,
                                         dots8[:, k:k + 1]).then_inc(row_used, 1)

            def keep_dots(r):
                dve.wait_ge(row_used, ROWS * r + ROWS)
                dve.tensor_copy(dots[:, bass.ds(ROWS * r, ROWS)], dots8[:, :]).then_inc(dots8_free, 1)

            def route_block(b, between=None):
                n = [0]
                gap = [0]

                def other():
                    if between is not None:
                        between(gap[0])
                    gap[0] += 1

                def begin():
                    wait(dve, route_step, ROUTE_STEPS * b + n[0])
                    dve.sem_inc(route_tick, 1)

                def step(ins):
                    ins.then_inc(route_step, 1)
                    n[0] += 1

                def top16(vals, idx, src, count):
                    for l in range(count):
                        ins = dve.max(vals[:, l, 0:8], src[:, l, :])
                    step(ins)
                    other()
                    begin()
                    for l in range(count):
                        ins = dve.max_index(idx[:, l, 0:8], vals[:, l, 0:8], src[:, l, :])
                    step(ins)
                    other()
                    begin()
                    for l in range(count):
                        ins = dve.match_replace(src[:, l, :], vals[:, l, 0:8], src[:, l, :], NEG_MAX)
                    step(ins)
                    other()
                    begin()
                    for l in range(count):
                        ins = dve.max(vals[:, l, 8:16], src[:, l, :])
                    step(ins)
                    other()
                    begin()
                    for l in range(count):
                        ins = dve.max_index(idx[:, l, 8:16], vals[:, l, 8:16], src[:, l, :])
                    step(ins)
                    other()
                    begin()

                begin()
                step(dve.tensor_copy(work[:, :, :], scores[:, bass.ds(b, 1), :, :].rearrange("p o l n -> p (o l) n")))
                begin()
                top16(best, best_i, work, LISTS)
                step(dve.tensor_copy(best_f[:, :, :], best_i[:, :, :]))
                halves = best[:, :, :].rearrange("p (h s) k -> p h s k", s=2)
                step(dve.tensor_tensor(cand[:, :, :].rearrange("p h (i j) -> p h i j", j=TOPK),
                                       halves[:, :, 0, :].unsqueeze(3).to_broadcast([P, PH, TOPK, TOPK]),
                                       halves[:, :, 1, :].unsqueeze(2).to_broadcast([P, PH, TOPK, TOPK]), ALU.add))
                begin()
                top16(top, top_i, cand, PH)
                flat_i = top_i[:, :, :].rearrange("p h k -> p (h k)")
                step(dve.tensor_scalar(pos_u[:, 0, :], flat_i, 4, None, ALU.logical_shift_right))
                step(dve.tensor_scalar(pos_u[:, 1, :], flat_i, TOPK - 1, None, ALU.bitwise_and))
                begin()
                step(dve.tensor_copy(pos_f[:, :, :], pos_u[:, :, :]))
                step(dve.tensor_tensor(sel[:, 2, bass.ds(b, 1), :].rearrange("p o (h k) -> p (o h) k", k=TOPK), top[:, :, :],
                                       top[:, :, 0:1].to_broadcast([P, PH, TOPK]), ALU.subtract))
                begin()
                ids = best_f[:, :, :].rearrange("p (h s) k -> p h s k", s=2)
                for s in range(2):
                    step(dve.tensor_tensor(match[:, :, :].rearrange("p h (k j) -> p (h k) j", j=TOPK),
                                           pos_f[:, s, :].unsqueeze(2).to_broadcast([P, P, TOPK]),
                                           iota[:, 0:TOPK].unsqueeze(1).to_broadcast([P, P, TOPK]), ALU.is_equal))
                    begin()
                    step(dve.tensor_tensor(prod[:, :, :].rearrange("p (h a) (k j) -> p h (a k) j", a=2, j=TOPK),
                                           match[:, :, :].rearrange("p h (k j) -> p h k j", j=TOPK),
                                           ids[:, :, s, :].unsqueeze(2).to_broadcast([P, PH, TOPK, TOPK]), ALU.mult))
                    begin()
                    ins = dve.tensor_reduce(sel[:, s, bass.ds(b, 1), :].rearrange("p o n -> p (o n)"),
                                            prod[:, :, :].rearrange("p l (k j) -> p (l k) j", j=TOPK), AX_X, ALU.add)
                    step(ins)
                    begin()
                ROUTE_SEEN[0] = n[0]

            ROUTE_SEEN = [0]
            dve.wait_ge(scores_ready, LISTS)
            route_block(0)
            dve.wait_ge(route_step, ROUTE_STEPS)
            dve.memset(dots8[:, :], 0.0).then_inc(dots8_free, 1)
            dve.scalar_tensor_tensor(expert[:, :], sel[:, 0, 0, :], float(NKEY), sel[:, 1, 0, :],
                                     ALU.mult, ALU.add).then_inc(expert_ready, 1)
            with dve.Fori(1, TB) as b:
                def two_dots(i):
                    if i < 8:
                        r = 2 * b + (i // 4 - 2)
                        for k in range(2 * (i % 4), 2 * (i % 4) + 2):
                            dot(k, r)
                        if i % 4 == 3:
                            keep_dots(r)
                route_block(b, two_dots)
            assert ROUTE_SEEN[0] == ROUTE_STEPS, ROUTE_SEEN

            gates = sel[:, 2, :, :].rearrange("p b (h k) -> p (b h) k", k=TOPK)
            dve.wait_ge(gate_exp, 1)
            dve.tensor_reduce(gsum[:, 0, :], gates, AX_X, ALU.add).then_inc(gate_step, 1)
            dve.wait_ge(gate_step, 1)
            dve.reciprocal(gsum[:, 1, :], gsum[:, 0, :]).then_inc(gate_step, 1)
            dve.wait_ge(gate_step, 2)
            dve.tensor_tensor(gates, gates, gsum[:, 1, :].unsqueeze(2).to_broadcast([P, TB * PH, TOPK]),
                              ALU.mult).then_inc(gates_ready, 1)
            dve.wait_ge(selT_ready, 3)
            dve.tensor_copy(gate_r[:, :], selT[:, 2, :]).then_inc(gate_step, 1)
            dve.wait_ge(gate_step, 3)
            dve.tensor_copy(gateT_hi[:, :], gate_r[:, :].bitcast(F32)).then_inc(gate_step, 1)
            dve.tensor_tensor(gateT_lo[:, :], selT[:, 2, :], gate_r[:, :].bitcast(F32), ALU.subtract).then_inc(gate_step, 1)
            dve.wait_ge(gate_step, 5)

            def one_hots(tile, o, first):
                slot = tile % 2
                if not first:
                    dve.wait_ge(scattered, 16 * o + (2 * tile - 2))
                if tile or not isinstance(o, int):
                    dve.wait_ge(onehot_ready, 8 * o + tile)
                t = bass.ds(2 * CHUNK * o + TOK_PER_TILE * tile, TOK_PER_TILE)
                shape = [P, TOK_PER_TILE, NKEY]
                row_of = iota[:, :].unsqueeze(1).to_broadcast(shape)

                def col(ap):
                    return ap.unsqueeze(2).to_broadcast(shape)

                dve.tensor_tensor(is_i1[:, :, :], row_of, col(selT[:, 0, t]), ALU.is_equal).then_inc(is_i1_ready, 1)
                dve.tensor_tensor(onehot[slot][0][:, :, :], row_of, col(selT[:, 1, t]), ALU.is_equal)
                dve.wait_ge(is_i1_ready, 8 * o + (tile + 1))
                dve.tensor_tensor(onehot[slot][1][:, :, :], is_i1[:, :, :], col(gateT_hi[:, t]), ALU.mult)
                dve.tensor_tensor(onehot[slot][2][:, :, :], is_i1[:, :, :], col(gateT_lo[:, t]),
                                  ALU.mult).then_inc(onehot_ready, 1)

            def two_chunks(o, first):
                for tile in range(8):
                    one_hots(tile, o, first and tile < 2)
                    dot(tile, o + R_PRE)
                keep_dots(o + R_PRE)

            two_chunks(0, True)
            with dve.Fori(1, O_MID) as o:
                two_chunks(o, False)
            for r in range(R_PRE + R_MID, R_ALL):
                for k in range(ROWS):
                    dot(k, r)
                keep_dots(r)
            dve.wait_ge(dots_gelu_ready, 1)
            dve.tensor_tensor(row_weight[:, :], dots_gelu[:, :], sel[:, 2, 0, :], ALU.mult).then_inc(row_weight_ready, 1)
            dve.tensor_scalar(x1[:, 0, :], x1[:, 0, :], ALPHA, None, ALU.mult).then_inc(residual_ready, 1)
            dve.wait_ge(row_weight_ready, 1)

            dve.wait_ge(g_stored[0], 16 * CHUNKS // 2)
            dve.wait_ge(g_stored[1], 16 * CHUNKS // 2)
            dve.memset(zeros[:, :].bitcast(F32), 0.0).then_inc(zeros_ready, 1)

            def weights(k, it, group, it_group, first):
                if k % 4 == 0:
                    dve.wait_ge(comb_loaded[group], 32 * it_group + 32)
                if not first:
                    dve.wait_ge(wgt_lo_ready, 4 * it + (k - 1))
                dve.tensor_tensor(wgt[k % 2][:, :].rearrange("p (c t) -> p c t", c=CHUNKS),
                                  ga[group][:, k % 4, :].rearrange("p (c t) -> p c t", c=CHUNKS),
                                  gg[group][:, :, k % 4, :], ALU.mult).then_inc(wgt_ready, 1)

            def weight_lo(k, it):
                dve.wait_ge(wgt_hi_ready, 4 * it + (k + 1))
                dve.tensor_tensor(wgt_lo[k % 2][:, :], wgt[k % 2][:, :], wgt_hi[k % 2][:, :].bitcast(F32),
                                  ALU.subtract).then_inc(wgt_lo_ready, 1)

            def add_row(k, r):
                dve.wait_ge(gathered[k], 16 * r + 16 * (R_ALL + 1))
                dve.wait_ge(row_used, ROWS * r + (RANKS + k))
                dve.scalar_tensor_tensor(x1[:, 0, :], rows[:, k, :], row_weight[:, bass.ds(ROWS * r + k, 1)],
                                         x1[:, 0, :], ALU.mult, ALU.add).then_inc(row_used, 1)

            for k in range(8):
                weights(k, 0, k // 4, 0, k < 2)
                if k == 0:
                    dve.wait_ge(residual_ready, 1)
                add_row(k, 0)
                weight_lo(k, 0)
            with dve.Fori(1, OCTETS) as i:
                for k in range(8):
                    weights(k, 2 * i, k // 4, i, False)
                    add_row(k, i)
                    weight_lo(k, 2 * i)

            dve.wait_ge(ln_loaded, 32)
            dve.wait_ge(row_used, 2 * RANKS)
            for b in range(TB):
                if b == 1:
                    dve.wait_ge(combined, 1)
                if b:
                    chained(dve.scalar_tensor_tensor(x1[:, b, :], x1[:, b, :], ALPHA,
                                                     banks[:, 2 * b:2 * b + 2, :].rearrange("p h n -> p (h n)"),
                                                     ALU.mult, ALU.add))
                layer_norm(b, x1[:, b, :], TB + b, None)
            for b in range(TB):
                finish_norm(b, x1[:, b, :], TB + b, ln2_gb, y_ready)

        @block.tensor
        def _(pe):
            pe.wait_ge(xT_loaded, 16)
            pe.wait_ge(small_loaded, 96)
            for k in range(KT):
                ins = pe.matmul(banks[0:HEADS, 2, :], ff_w[:, k, :], xT[:, k, :], start=(k == 0), stop=(k == KT - 1))
            ins.then_inc(ff_ready, 1)
            pe.wait_ge(xT_split, 2)

            def features(c, it, bank, hiT, loT, part=0, parts=1, tokens=slice(0, SEQ)):
                if part == 0:
                    pe.wait_ge(lo_ready, 4 * it + (c + 1))
                h, l = hi[c % PART_SLOTS], lo[c % PART_SLOTS]
                o = banks[:, bank, 0:tokens.stop - tokens.start]
                for k in range(part * KT // parts, (part + 1) * KT // parts):
                    s = bass.ts(k, P)
                    pe.matmul(o, h[:, s], hiT[:, k, tokens], start=(k == 0), stop=False)
                    pe.matmul(o, h[:, s], loT[:, k, tokens], start=False, stop=False)
                    ins = pe.matmul(o, l[:, s], hiT[:, k, tokens], start=False, stop=(k == KT - 1))
                if part == parts - 1:
                    ins.then_inc(tile_used, 1)

            def values(c, it, bank, part=0, parts=1):
                if part == 0:
                    pe.wait_ge(lo_ready, 4 * it + (c + 1))
                h, l = hi[c % PART_SLOTS], lo[c % PART_SLOTS]
                for n in range(part * TB * KT // parts, (part + 1) * TB * KT // parts):
                    b, k = divmod(n, KT)
                    o, s, t = banks[:, bank, bass.ts(b, P)], bass.ts(k, P), bass.ts(b, P)
                    pe.matmul(o, xT_hi[:, k, t], h[:, s], start=(k == 0), stop=False)
                    pe.matmul(o, xT_hi[:, k, t], l[:, s], start=False, stop=False)
                    ins = pe.matmul(o, xT_lo[:, k, t], h[:, s], start=False, stop=(k == KT - 1))
                if part == parts - 1:
                    ins.then_inc(tile_used, 1)

            features(0, 0, 0, xT_hi, xT_lo)
            values(1, 0, 1)
            pe.wait_ge(consts_ready, 4)

            def project(k, j, part=0, parts=1):
                if part == 0:
                    pe.wait_ge(proj_copied, 4 * j + (k + 1))
                if k == 2:
                    values(S_LOOP + k, j, k % 2, part, parts)
                else:
                    features(S_LOOP + k, j, k % 2, xT_hi, xT_lo, part, parts)

            for k in range(4):
                project(k, 0)

            def pair(j, last):
                def logits(u):
                    kind, a, qb, k0, nk = UNITS[u]
                    hs = slice(a * HD, (a + 1) * HD)
                    qs = bass.ts(qb, P)
                    o = banks[:, 2 + u % 2, 0:nk * P]
                    if u >= 2:
                        pe.wait_ge(exp_ready, NU * j + (u - 1))
                    if u == 0:
                        pe.wait_ge(proj_copied, 4 * j + 4)
                        pe.wait_ge(decay_loaded, 32 * j + 32)
                    if u == SWA_UNITS:
                        pe.wait_ge(proj_copied, 4 * j + 6)
                    if kind == "fox":
                        pe.matmul(o, qT[hs, qs], kT[hs, 0:nk * P], start=True, stop=False)
                        pe.matmul(o, decay_q[:, a, qs], decay_k[:, a, 0:nk * P], start=False, stop=False)
                        pe.matmul(o, ident_r[:, :], mask_r[:, (4 - nk) * P:], start=False, stop=True).then_inc(logits_ready, 1)
                    else:
                        pe.matmul(o, swa_q[hs, qs], swa_k[hs, k0 * P:(k0 + nk) * P], start=True, stop=False)
                        pe.matmul(o, ident_r[:, :],
                                  bias_r[:, bass.ds(2 * j + a, 1), (2 - nk) * P:].rearrange("p o k -> p (o k)"),
                                  start=False, stop=True).then_inc(logits_ready, 1)

                def turn(u):
                    kind, a, qb, k0, nk = UNITS[u]
                    pe.wait_ge(probs_ready, NU * j + (u + 1))
                    if u >= 2:
                        pe.wait_ge(turned_copied, NU * j + (u - 1))
                    for k in range(nk):
                        ins = pe.transpose(banks[:, 4 + u % 2, bass.ts(k, P)], probs[u % 3][:, bass.ts(k, P)], ident[:, :])
                    ins.then_inc(turned, 1)

                def mix(u):
                    kind, a, qb, k0, nk = UNITS[u]
                    hs = slice(a * HD, (a + 1) * HD)
                    pe.wait_ge(turned_copied, NU * j + (u + 1))
                    if u == 0:
                        pe.wait_ge(proj_copied, 4 * j + 5)
                    o = banks[hs, 6 + (kind == "swa"), bass.ts(qb, P)]
                    val = vv if kind == "fox" else swa_v
                    for k in range(nk):
                        ins = pe.matmul(o, val[:, k0 + k, hs], probs_t[u % 2][:, k, :], start=(k == 0), stop=(k == nk - 1))
                    ins.then_inc(head_mixed, 1)

                for step in range(STEPS):
                    if step < NU:
                        logits(step)
                    if 0 <= step - TURN_LAG < NU:
                        turn(step - TURN_LAG)
                    if 0 <= step - MIX_LAG:
                        mix(step - MIX_LAG)
                    for first, (k, n) in PROJ_AT.items():
                        if not last and first <= step < first + n:
                            project(k, j + 1, step - first, n)

            with pe.Fori(0, PAIRS - 1) as j:
                pair(j, False)
            pair(PAIRS - 1, True)

            def combine(c, it, h_at, l_at, start, stop, first_block=0):
                h, l = hi[c % PART_SLOTS], lo[c % PART_SLOTS]
                for b in range(first_block, TB):
                    for n in range(2):
                        o, s = banks[:, 2 * b + n, :], bass.ts(n, 512)
                        pe.matmul(o, h_at(b), h[:, s], start=start, stop=False)
                        pe.matmul(o, h_at(b), l[:, s], start=False, stop=False)
                        ins = pe.matmul(o, l_at(b), h[:, s], start=False, stop=stop)
                ins.then_inc(tile_used, 1)
                return ins

            pe.wait_ge(mix_lo_ready, 2 * PAIRS)
            for r in range(KT):
                pe.wait_ge(lo_ready, S_WOUT + r + 1)
                combine(S_WOUT + r, 0, lambda b: mix_hi[:, r, bass.ts(b, P)], lambda b: mix_lo[:, r, bass.ts(b, P)],
                        r == 0, r == KT - 1)

            for b in range(TB):
                pe.wait_ge(x1_ready, b + 1)
                for k in range(KT):
                    ins = pe.transpose(banks[:, 2 * b + k // 4, bass.ts(k % 4, P)], x1[:, b, bass.ts(k, P)], ident[:, :])
                ins.then_inc(x1_turned, 1)

            pe.wait_ge(x1T_lo_ready, TB)
            pe.wait_ge(keys_loaded, 16)

            def score(l, it):
                pe.wait_ge(qh_ready, 4 * it + (l + 1))
                wait(pe, scores_ready, 4 * it + (l - 1))
                for b in range(TB):
                    ins = pe.matmul(banks[:, 2 + l % 2, bass.ts(b, P)], qh[l % 2][:, bass.ts(b, P)],
                                    keys[:, bass.ds(4 * it + l, 1), :].rearrange("p o n -> p (o n)"),
                                    start=True, stop=True)
                ins.then_inc(scored, 1)

            def query_group(it):
                for l in range(4):
                    wait(pe, qh_ready, 4 * it + (l - 1))
                    features(S_PQ + l, it, l % 2, x1T_hi, x1T_lo)
                    score(l, it)

            query_group(0)
            with pe.Fori(1, LISTS // 4) as it:
                query_group(it)

            def expert_tile(k, it, first=False):
                if first:
                    pe.wait_ge(qh_ready, LISTS)
                else:
                    pe.wait_ge(gelu_ready, 4 * it + (k - 1))
                features(S_U + k, it, k % 2, x1T_hi, x1T_lo, tokens=slice(P, SEQ))

            for k in range(4):
                expert_tile(k, 0, first=k < 2)
            with pe.Fori(1, A_PRE // 4) as it:
                for k in range(4):
                    expert_tile(k, it)

            pe.wait_ge(gates_ready, 1)
            for m in range(3):
                for b in range(1, TB):
                    ins = pe.transpose(banks[:, 2 + m, bass.ts(b - 1, P)], sel[:, m, b, :], ident[:, :])
                ins.then_inc(sel_turned, 1)
            pe.wait_ge(selT_ready, 3)

            def scatter(tile, o, first):
                slot = tile % 2
                pe.wait_ge(onehot_ready, 8 * o + (tile + 1))
                for g in range(2):
                    if not first:
                        pe.wait_ge(staged, 16 * o + (2 * tile + g - 1))
                    for k in range(4 * g, 4 * g + 4):
                        r = banks[:, 2 + g, bass.ts(k % 4, NKEY)]
                        pe.matmul(r, onehot[slot][0][:, k, :], onehot[slot][1][:, k, :], start=True, stop=False)
                        ins = pe.matmul(r, onehot[slot][0][:, k, :], onehot[slot][2][:, k, :], start=False, stop=True)
                    ins.then_inc(scattered, 1)

            def two_chunks(o, first):
                for tile in range(8):
                    expert_tile(tile % 4, 2 * o + (A_PRE // 4 + tile // 4))
                    scatter(tile, o, first and tile == 0)

            two_chunks(0, True)
            with pe.Fori(1, O_MID) as o:
                two_chunks(o, False)
            for it in range((A_PRE + A_MID) // 4, ETILES // 4):
                for k in range(4):
                    expert_tile(k, it)

            pe.wait_ge(gelu_ready, ETILES)
            pe.wait_ge(staged, DENSE // 4)
            pe.wait_ge(zeros_ready, 1)
            for n in range(2, 8):
                pe.matmul(banks[:, n, :], zeros[:, 0:P], zeros[:, :], start=True, stop=False)

            def experts(k, it):
                pe.wait_ge(lo_ready, 4 * it + (S_V + k + 1))
                pe.wait_ge(wgt_lo_ready, 4 * it + (k + 1))
                slot = k % 2
                combine(S_V + k, it, lambda b: wgt_hi[slot][:, bass.ts(b - 1, P)],
                        lambda b: wgt_lo[slot][:, bass.ts(b - 1, P)], False, False, first_block=1)

            with pe.Fori(0, ETILES // 8) as i:
                for k in range(8):
                    experts(k, 2 * i)
            for n in range(2, 8):
                ins = pe.matmul(banks[:, n, :], zeros[:, 0:P], zeros[:, :], start=False, stop=True)
            ins.then_inc(combined, 1)


def kernel(x, ln1_g, ln1_b, w_in, b_f, sink, w_out, ln2_g, ln2_b, w_pq, peer_keys1, peer_keys2, peer_u, peer_v):
    import numpy as np
    import concourse.bacc as bacc
    from concourse.bass_utils import run_bass_kernel_spmd

    def tiles(w):
        n = w.shape[1] // P
        return np.ascontiguousarray(w.reshape(KT, P, n, P).transpose(2, 1, 0, 3)).reshape(n, P, D)

    x, w_in, w_out = np.asarray(x)[0], np.asarray(w_in)[0], np.asarray(w_out)[0]
    fox_q, fox_k, fox_v, w_f, swa_q, swa_k, swa_v = np.split(w_in, [512, 1024, 1536, 1544, 2056, 2184], axis=1)
    order = [h for j in range(PAIRS) for h in (j, PAIRS + j)]
    swa_q = swa_q.reshape(D, HEADS, HD)[:, order].reshape(D, HEADS * HD)
    swa_rows = w_out[512:].reshape(HEADS, HD, D)[order].reshape(HEADS * HD, D)
    fq, fk, fv, sq = tiles(fox_q), tiles(fox_k), tiles(fox_v), tiles(swa_q)
    looped = [t[j] for j in range(PAIRS) for t in (fq, fk, fv, sq)]
    w1 = np.stack([tiles(swa_k)[0], tiles(swa_v)[0], *looped, *w_out[:512].reshape(4, P, D), *swa_rows.reshape(4, P, D)])

    blocked = -2.0 ** 100
    i = np.arange(P)
    mask = np.zeros((P, 4 * P), np.float32)
    mask[:, 3 * P:] = np.where(i[None, :] <= i[:, None], 0.0, blocked)
    key = np.arange(SWA_KEYS)[None, :] - P
    chunks_back = i[:, None] // 64 - key // 64
    seen = (chunks_back >= 0) & (chunks_back <= 1)
    slopes = 2.0 ** -(np.array(order) + 1.0)
    bias = np.where(seen[:, None, :], -slopes[None, :, None] * np.abs(i[:, None] - key)[:, None, :], blocked)
    consts = np.concatenate([mask, bias.reshape(P, -1), np.eye(P), np.tile(i, (P, 1))], axis=1).astype(np.float32)

    keys = np.stack([np.asarray(peer_keys1)[0], np.asarray(peer_keys2)[0]], axis=1).reshape(LISTS, NKEY, P)
    u = np.asarray(peer_u)[0]
    arrays = {
        "x_t": x.T.reshape(KT, P, SEQ).transpose(1, 0, 2),
        "x_rows": x.reshape(TB, P, D).transpose(1, 0, 2),
        "w1": w1,
        "w_ff": w_f.reshape(KT, P, HEADS).transpose(1, 0, 2),
        "b_f": np.asarray(b_f).reshape(HEADS, 1),
        "sinks": np.broadcast_to(np.asarray(sink)[0][order], (P, HEADS)),
        "ln_par": np.broadcast_to(np.stack([np.asarray(a)[0] for a in (ln1_g, ln1_b, ln2_g, ln2_b)]), (P, 4, D)),
        "w_pq": tiles(np.asarray(w_pq)[0]),
        "keys_t": keys.transpose(2, 0, 1),
        "u_t": u.reshape(ETILES, P, KT, P).transpose(0, 3, 2, 1).reshape(ETILES, P, D),
        "u_rows": u,
        "v_tab": np.asarray(peer_v)[0].reshape(ETILES, P, D),
        "consts": consts,
    }
    arrays = {n: np.ascontiguousarray(a) for n, a in arrays.items()}
    nc = bacc.Bacc("TRN2", target_bir_lowering=False, num_devices=1)
    args = [nc.dram_tensor(n, a.shape, F32, kind="ExternalInput").ap() for n, a in arrays.items()]
    args.append(nc.dram_tensor("out", (SEQ, D), F32, kind="ExternalOutput").ap())
    build(nc, *args)
    r = run_bass_kernel_spmd(nc, [arrays], core_ids=[0])
    return r.results[0]["out"].reshape(1, SEQ, D)
```

```python
from contextlib import ExitStack

import concourse.bass as bass
from concourse import mybir

F32 = mybir.dt.float32
F32R = mybir.dt.float32r
U32 = mybir.dt.uint32
ALU = mybir.AluOpType
ACT = mybir.ActivationFunctionType
AX_X = mybir.AxisListType.X

P = 128
SEQ = 512
D = 1024
KT = D // P
TB = SEQ // P
HEADS = 8
PAIRS = HEADS // 2
HD = 64
SWA_KEYS = 2 * P
LISTS = 16
PH = 8
TOPK = 16
NKEY = 128
ETILES = 128
EPS = 1e-5
ALPHA = 2.0 ** 0.25
NEG_MAX = -3.0e38

RAW_SLOTS = 4
PART_SLOTS = 2
S_LOOP = 2
S_WOUT = S_LOOP + 4 * PAIRS
S_WOUT_B = S_WOUT + KT
S_PQ = S_WOUT_B + KT
S_U = S_PQ + LISTS
S_V = S_U + ETILES
N_TILES = S_V + ETILES

DENSE = SEQ - P
RANKS = PH * TOPK
ROWS = 8

OCTETS = ETILES // 8
O_IDLE = 2
TOK_PER_TILE = 8
CHUNK = 32
TILES_PER_CHUNK = CHUNK // TOK_PER_TILE
CHUNKS = DENSE // CHUNK
O_MID = CHUNKS // 2
A_PRE = 68
A_MID = 8 * O_MID
A_POST = ETILES - A_PRE - A_MID
R_PRE = 6
R_MID = O_MID
H_DOT = 4
R_ALL = RANKS // ROWS
AHEAD = 4
ROUTE_STEPS = 1 + 5 + 2 + 5 + 2 + 2 + 6
X_CHUNKS = 4


def build(nc, x_t, x_rows, w1, w_ff, b_f, sinks, ln_par, w_pq, keys_t, u_t, u_rows, v_tab, consts, out):
    g_dram = nc.dram_tensor("g_scratch", (CHUNKS, P, ETILES, CHUNK), F32, kind="Internal").ap()
    a_dram = nc.dram_tensor("gelu_scratch", (ETILES // 4, P, 4, DENSE), F32, kind="Internal").ap()
    c_dram = nc.dram_tensor("decay_scratch", (4, HEADS, SEQ), F32R, kind="Internal").ap()

    ctx = ExitStack()
    with ctx:
        def sb(name, shape, dt=F32, stack=ctx):
            return stack.enter_context(nc.sbuf_tensor(name, shape, dt))

        def sem(name):
            return ctx.enter_context(nc.semaphore(name))

        raw = sb("raw", [P, RAW_SLOTS, D])
        hi = [sb(f"hi{i}", [P, D], F32R) for i in range(PART_SLOTS)]
        lo = [sb(f"lo{i}", [P, D], F32R) for i in range(PART_SLOTS)]
        x1 = sb("x1", [P, TB, D])
        ident = sb("ident", [P, P])
        iota = sb("iota", [P, NKEY])
        stats = sb("stats", [P, TB, 2, 6])
        moments = sb("moments", [P, TB, 2])
        rstd = sb("rstd", [P, TB, 6])

        att = ExitStack()
        xT_hi = sb("xT_hi", [P, KT, SEQ], F32R, att)
        xT_lo = sb("xT_lo", [P, KT, SEQ], F32R, att)
        xbuf = sb("xbuf", [P, KT * SEQ], F32, att)
        xT = xbuf[:, :].rearrange("p (k t) -> p k t", k=KT)
        xR = xbuf[:, :].rearrange("p (b d) -> p b d", b=TB)
        ff_w = sb("ff_w", [P, KT, HEADS], F32, att)
        ff_b = sb("ff_b", [HEADS, 1], F32, att)
        sink = sb("sink", [P, HEADS], F32, att)
        neg_sink = sb("neg_sink", [P, HEADS], F32, att)
        cst = sb("cst", [P, P + HEADS * SWA_KEYS], F32, att)
        ident_r = sb("ident_r", [P, P], F32R, att)
        mask_r = sb("mask_r", [P, P], F32R, att)
        bias_r = sb("bias_r", [P, HEADS, SWA_KEYS], F32R, att)
        ff = [sb(f"ff{i}", [HEADS, SEQ], F32, att) for i in range(4)]
        decay_r = sb("decay_r", [HEADS, 4, SEQ], F32R, att)
        decay_q = sb("decay_q", [4, 2, SEQ], F32R, att)
        decay_k = sb("decay_k", [4, 2, SEQ], F32R, att)
        qT = sb("qT", [P, SEQ], F32, att)
        kT = sb("kT", [P, SEQ], F32, att)
        vT = sb("vT", [P, SEQ], F32, att)
        vv = sb("vv", [P, TB, P], F32, att)
        swa_q = sb("swa_q", [P, SEQ], F32, att)
        swa_k = sb("swa_k", [P, SEQ], F32, att)
        swa_v = sb("swa_v", [P, TB, P], F32, att)
        probs = [sb(f"probs{i}", [P, SEQ], F32, att) for i in range(3)]
        probs_t = [sb(f"probs_t{i}", [P, 4, P], F32, att) for i in range(2)]
        row = [sb(f"row{i}", [P, 8], F32, att) for i in range(3)]
        mix_hi = sb("mix_hi", [P, KT, SEQ], F32R, att)
        mix_lo = sb("mix_lo", [P, KT, SEQ], F32R, att)
        ln1_gb = sb("ln1_gb", [P, 2, D], F32, att)
        att.close()

        x1T_hi = sb("x1T_hi", [P, KT, SEQ], F32R)
        x1T_lo = sb("x1T_lo", [P, KT, SEQ], F32R)
        sel = sb("sel", [P, 3, TB, P])
        selT = sb("selT", [P, 3, DENSE])
        gateT_hi = sb("gateT_hi", [P, DENSE])
        gateT_lo = sb("gateT_lo", [P, DENSE])
        gate_r = sb("gate_r", [P, DENSE], F32R)
        gelu = [sb(f"gelu{i}", [P, DENSE]) for i in range(2)]
        rows = sb("rows", [P, ROWS, D])
        expert = sb("expert", [P, RANKS], U32)
        expert_at = [sb(f"expert_at{i}", [P, 1], U32) for i in range(ROWS)]
        dots8 = sb("dots8", [P, ROWS])
        dots = sb("dots", [P, RANKS])
        dots_gelu = sb("dots_gelu", [P, RANKS])
        row_weight = sb("row_weight", [P, RANKS])
        route = ExitStack()
        keys = sb("keys", [P, LISTS, NKEY], F32, route)
        qh = [sb(f"qh{i}", [P, SEQ], F32, route) for i in range(2)]
        scores = sb("scores", [P, TB, LISTS, NKEY], F32, route)
        work = sb("work", [P, LISTS, NKEY], F32, route)
        best = sb("best", [P, LISTS, TOPK], F32, route)
        best_i = sb("best_i", [P, LISTS, TOPK], U32, route)
        best_f = sb("best_f", [P, LISTS, TOPK], F32, route)
        cand = sb("cand", [P, PH, TOPK * TOPK], F32, route)
        match = cand
        prod = work
        top = sb("top", [P, PH, TOPK], F32, route)
        top_i = sb("top_i", [P, PH, TOPK], U32, route)
        pos_u = sb("pos_u", [P, 2, P], U32, route)
        pos_f = sb("pos_f", [P, 2, P], F32, route)
        gsum = sb("gsum", [P, 2, TB * PH], F32, route)
        route.close()
        scat = ExitStack()
        onehot = [[sb(f"onehot{i}_{j}", [P, TOK_PER_TILE, NKEY], F32R, scat) for j in range(3)] for i in range(2)]
        is_i1 = sb("is_i1", [P, TOK_PER_TILE, NKEY], F32, scat)
        stage = [sb(f"stage{i}", [P, ETILES, CHUNK], F32, scat) for i in range(2)]
        scat.close()
        kept = sb("kept", [P, A_POST, DENSE])
        comb = ExitStack()
        ga = [sb(f"ga{i}", [P, 4, DENSE], F32, comb) for i in range(2)]
        gg = [sb(f"gg{i}", [P, CHUNKS, 4, CHUNK], F32, comb) for i in range(2)]
        wgt = [sb(f"wgt{i}", [P, DENSE], F32, comb) for i in range(2)]
        wgt_hi = [sb(f"wgt_hi{i}", [P, DENSE], F32R, comb) for i in range(2)]
        wgt_lo = [sb(f"wgt_lo{i}", [P, DENSE], F32R, comb) for i in range(2)]
        ln2_gb = sb("ln2_gb", [P, 2, D], F32, comb)
        comb.close()

        banks = ctx.enter_context(nc.psum_tensor("banks", [P, 8, 512], F32))

        raw_loaded = [sem(f"raw_loaded{i}") for i in range(RAW_SLOTS)]
        hi_ready = sem("hi_ready")
        lo_ready = sem("lo_ready")
        tile_used = sem("tile_used")
        xT_loaded = [sem(f"xT_loaded{i}") for i in range(X_CHUNKS)]
        ff_loaded = sem("ff_loaded")
        small_loaded = sem("small_loaded")
        xR_loaded = sem("xR_loaded")
        ln_loaded = sem("ln_loaded")
        xT_hi_ready = sem("xT_hi_ready")
        xT_lo_ready = sem("xT_lo_ready")
        consts_ready = sem("consts_ready")
        ff_ready = sem("ff_ready")
        ff_step = sem("ff_step")
        decay_ready = sem("decay_ready")
        decay_stored = sem("decay_stored")
        decay_loaded = sem("decay_loaded")
        proj_copied = sem("proj_copied")
        v_turned = sem("v_turned")
        logits_ready = sem("logits_ready")
        max_step = sem("max_step")
        max_ready = sem("max_ready")
        exp_ready = sem("exp_ready")
        norm_step = sem("norm_step")
        probs_ready = sem("probs_ready")
        turned = sem("turned")
        turned_copied = sem("turned_copied")
        head_mixed = sem("head_mixed")
        mix_hi_ready = sem("mix_hi_ready")
        mix_lo_ready = sem("mix_lo_ready")
        block_mixed = sem("block_mixed")
        ln_step = sem("ln_step")
        sqrt_ready = sem("sqrt_ready")
        norm_chain = sem("norm_chain")
        factors_ready = sem("factors_ready")
        scaled = sem("scaled")
        shift_chain = sem("shift_chain")
        shared_done = sem("shared_done")
        x1_ready = sem("x1_ready")
        x1_turned = sem("x1_turned")
        x1T_hi_ready = sem("x1T_hi_ready")
        x1T_lo_ready = sem("x1T_lo_ready")
        keys_loaded = sem("keys_loaded")
        qh_ready = sem("qh_ready")
        scored = sem("scored")
        scores_ready = sem("scores_ready")
        route_step = sem("route_step")
        route_tick = sem("route_tick")
        gate_exp = sem("gate_exp")
        gate_step = sem("gate_step")
        gates_ready = sem("gates_ready")
        sel_turned = sem("sel_turned")
        selT_ready = sem("selT_ready")
        gelu_ready = sem("gelu_ready")
        expert_ready = sem("expert_ready")
        expert_at_ready = sem("expert_at_ready")
        gathered = [sem(f"gathered{i}") for i in range(ROWS)]
        row_used = sem("row_used")
        dots8_free = sem("dots8_free")
        dots_gelu_ready = sem("dots_gelu_ready")
        residual_ready = sem("residual_ready")
        row_weight_ready = sem("row_weight_ready")
        gelu_stored = [sem(f"gelu_stored{i}") for i in range(2)]
        onehot_ready = sem("onehot_ready")
        is_i1_ready = sem("is_i1_ready")
        scattered = sem("scattered")
        staged = sem("staged")
        g_stored = [sem(f"g_stored{i}") for i in range(2)]
        comb_loaded = [sem(f"comb_loaded{i}") for i in range(2)]
        wgt_ready = sem("wgt_ready")
        wgt_hi_ready = sem("wgt_hi_ready")
        wgt_lo_ready = sem("wgt_lo_ready")
        combined = sem("combined")
        y_ready = sem("y_ready")
        out_stored = sem("out_stored")

        def wait(eng, s, value):
            if not (isinstance(value, int) and value <= 0):
                eng.wait_ge(s, value)

        def x_chunk(i):
            return slice(i * KT // X_CHUNKS, (i + 1) * KT // X_CHUNKS)

        def pair_copies(j):
            return 5 * j + 3


        def load_tile(eng, c, it, src):
            wait(eng, lo_ready, 4 * it + (c - RAW_SLOTS + 1))
            eng.dma_start(raw[:, c % RAW_SLOTS, :], src).then_inc(raw_loaded[c % RAW_SLOTS], 16)

        def split_hi(act, c, it):
            wait(act, raw_loaded[c % RAW_SLOTS], 16 * it + 16 * (c // RAW_SLOTS + 1))
            wait(act, tile_used, 4 * it + (c - PART_SLOTS + 1))
            act.activation(hi[c % PART_SLOTS][:, :], raw[:, c % RAW_SLOTS, :], ACT.Copy).then_inc(hi_ready, 1)

        def split_lo(eng, c, it):
            wait(eng, hi_ready, 4 * it + (c + 1))
            eng.tensor_tensor(lo[c % PART_SLOTS][:, :], raw[:, c % RAW_SLOTS, :],
                              hi[c % PART_SLOTS][:, :].bitcast(F32), ALU.subtract).then_inc(lo_ready, 1)

        def units():
            for a in range(2):
                for qb in range(TB):
                    yield "fox", a, qb, 0, qb + 1
            for a in range(2):
                for qb in range(TB):
                    yield "swa", a, qb, max(qb - 1, 0), min(qb, 1) + 1

        KEPT = A_POST // 4
        KEPT_FROM = ETILES // 4 - KEPT

        UNITS = list(units())
        NU = len(UNITS)
        SWA_UNITS = NU // 2

        TURN_LAG, MIX_LAG = 2, 3
        STEPS = NU + MIX_LAG
        OUTPUT_AT = 2
        PROJ_AT = {8: (0, 3), 11: (1, 3), 14: (2, 3), 17: (3, 2)}

        TURN_AT = 5

        SHARED_X, SHARED_Y = (2,), (0, 1, 2)
        SHARED = [b for b in SHARED_X] + [TB + b for b in SHARED_Y]

        def shared_norm(n):
            return SHARED.index(n)

        def count_swa(u):
            return sum(1 for k in UNITS[:u] if k[0] == "swa")

        block = ctx.enter_context(nc.Block())

        @block.sync
        def _(sp):
            sp.dma_start(ff_w[:, :, :], w_ff).then_inc(ff_loaded, 16)
            for i in range(X_CHUNKS):
                sp.dma_start(xT[:, x_chunk(i), :], x_t[:, x_chunk(i), :]).then_inc(xT_loaded[i], 16)
            for c in range(S_LOOP):
                load_tile(sp, c, 0, w1[c])
            sp.dma_start(ff_b[:, :], b_f).then_inc(ff_loaded, 16)
            sp.dma_start(cst[:, :], consts[:, 0:P + HEADS * SWA_KEYS]).then_inc(small_loaded, 16)
            sp.dma_start(ident[:, :], consts[:, P + HEADS * SWA_KEYS:2 * P + HEADS * SWA_KEYS]).then_inc(small_loaded, 16)
            sp.dma_start(iota[:, :], consts[:, 2 * P + HEADS * SWA_KEYS:]).then_inc(small_loaded, 16)
            sp.dma_start(sink[:, :], sinks).then_inc(small_loaded, 16)
            sp.dma_start(ln1_gb[:, :, :], ln_par[:, 0:2, :]).then_inc(ln_loaded, 16)
            for c in range(S_LOOP, S_LOOP + 4):
                load_tile(sp, c, 0, w1[c])
            with sp.Fori(1, PAIRS) as j:
                for k in range(4):
                    load_tile(sp, S_LOOP + k, j, w1[4 * j + (S_LOOP + k)])
            sp.wait_ge(xT_lo_ready, X_CHUNKS)
            sp.wait_ge(ff_ready, 1)
            sp.dma_start(xR, x_rows).then_inc(xR_loaded, 16)
            for c in range(S_WOUT, S_PQ):
                load_tile(sp, c, 0, w1[S_WOUT + (c - S_WOUT) % KT])
            for c in range(S_PQ, S_PQ + 4):
                load_tile(sp, c, 0, w_pq[c - S_PQ])
            sp.wait_ge(x1T_lo_ready, TB)
            sp.dma_start(keys[:, :, :], keys_t).then_inc(keys_loaded, 16)
            with sp.Fori(1, LISTS // 4) as i:
                for k in range(4):
                    load_tile(sp, S_PQ + k, i, w_pq[4 * i + k])

            def store_gelu(slot, n_it, k, value):
                sp.wait_ge(gelu_ready, value)
                sp.dma_start(a_dram[n_it, :, k, :], gelu[slot][:, :]).then_inc(gelu_stored[slot], 16)

            for k in range(4):
                load_tile(sp, S_U + k, 0, u_t[k])

            def tiles_and_stores(it):
                for k in range(4):
                    load_tile(sp, S_U + 4 + k, it, u_t[4 * it + (4 + k)])
                    store_gelu(k % 2, it, k, 4 * it + (k + 1))

            with sp.Fori(0, A_PRE // 4) as it:
                tiles_and_stores(it)
            with sp.Fori(0, O_MID) as o:
                for half in range(2):
                    tiles_and_stores(2 * o + (A_PRE // 4 + half))
                    sp.wait_ge(staged, 4 * TILES_PER_CHUNK * o + 2 * TILES_PER_CHUNK * (half + 1))
                    sp.dma_start(g_dram[2 * o + half], stage[half][:, :, :]).then_inc(g_stored[half], 16)
            for it in range((A_PRE + A_MID) // 4, ETILES // 4 - 1):
                for k in range(4):
                    load_tile(sp, S_U + 4 + k, it, u_t[4 * it + (4 + k)])
            for half in range(2):
                sp.wait_ge(gelu_stored[half], 16 * (A_PRE + A_MID) // 2)
                sp.wait_ge(g_stored[half], 16 * CHUNKS // 2)

            def load_group(g, slot):
                if not (isinstance(g, int) and g >= KEPT_FROM):
                    sp.dma_start(ga[slot][:, :, :], a_dram[g]).then_inc(comb_loaded[slot], 16)
                sp.dma_start(gg[slot][:, :, :, :],
                             g_dram[:, :, bass.ds(4 * g, 4), :].rearrange("c p n t -> p c n t")
                             ).then_inc(comb_loaded[slot], 16)

            load_group(KEPT_FROM, 0)
            load_group(KEPT_FROM + 1, 1)
            for k in range(8):
                load_tile(sp, S_V + k, 0, v_tab[4 * KEPT_FROM + k])
            sp.dma_start(ln2_gb[:, :, :], ln_par[:, 2:4, :]).then_inc(ln_loaded, 16)
            for slot, g in enumerate((KEPT_FROM + 2, 0)):
                sp.wait_ge(wgt_ready, 4 * slot + 4)
                load_group(g, slot)
                for k in range(4):
                    load_tile(sp, S_V + 8 + 4 * slot + k, 0, v_tab[4 * g + k])
            with sp.Fori(2, ETILES // 8) as i:
                for slot in range(2):
                    sp.wait_ge(wgt_ready, 8 * i + (4 * slot - 4))
                    load_group(2 * i + (slot - KEPT), slot)
                    for k in range(4):
                        load_tile(sp, S_V + 4 * slot + k, 2 * i, v_tab[8 * i + (4 * (slot - KEPT) + k)])
            for b in (0, 1, 3, 2):
                if b in SHARED_Y:
                    sp.wait_ge(shared_done, shared_norm(TB + b) + 1)
                else:
                    sp.wait_ge(y_ready, 1)
                sp.dma_start(out[bass.ts(b, P), :], x1[:, b, :]).then_inc(out_stored, 16)
            sp.wait_ge(out_stored, 16 * TB)

        @block.gpsimd
        def _(pool):
            pool.memset(decay_q[:, :, :].bitcast(F32), 1.0).then_inc(decay_ready, 1)
            pool.memset(decay_k[:, :, :].bitcast(F32), 1.0).then_inc(decay_ready, 1)
            for c in range(S_LOOP):
                split_lo(pool, c, 0)
            for k in range(2):
                split_lo(pool, S_LOOP + k, 0)
            pool.wait_ge(decay_ready, 6)
            pool.dma_start(c_dram.rearrange("r h t -> h r t"), decay_r[:, :, :]).then_inc(decay_stored, 16)
            split_lo(pool, S_LOOP + 2, 0)
            pool.wait_ge(decay_stored, 16)

            def load_decay(j):
                pool.dma_start(decay_q[2:4, :, :], c_dram[0:2, bass.ds(2 * j, 2), :]).then_inc(decay_loaded, 16)
                pool.dma_start(decay_k[0:2, :, :], c_dram[2:4, bass.ds(2 * j, 2), :]).then_inc(decay_loaded, 16)

            load_decay(0)
            for k in range(3, 6):
                split_lo(pool, S_LOOP + k, 0)
            with pool.Fori(0, PAIRS - 1) as j:
                pool.wait_ge(logits_ready, NU * j + SWA_UNITS)
                load_decay(j + 1)
                for k in range(6, 10):
                    split_lo(pool, S_LOOP + k, j)
            for c in range(S_WOUT + 2, S_PQ):
                split_lo(pool, c, 0)

            def gain_and_bias(n, gb):
                b, i = n % TB, shared_norm(n)
                pool.wait_ge(scaled, i + 1)
                pool.tensor_tensor(x1[:, b, :], x1[:, b, :], gb[:, 0, :], ALU.mult).then_inc(shift_chain, 1)
                pool.wait_ge(shift_chain, i + 1)
                pool.tensor_tensor(x1[:, b, :], x1[:, b, :], gb[:, 1, :], ALU.add).then_inc(shared_done, 1)

            for k in range(8):
                split_lo(pool, S_PQ + k, 0)
                if k == 1:
                    gain_and_bias(2, ln1_gb)
            with pool.Fori(1, (S_U - S_PQ) // 8 + O_IDLE) as o:
                for k in range(8):
                    split_lo(pool, S_PQ + k, 2 * o)

            v_rows = v_tab.rearrange("n p d -> (n p) d")

            def gather(table, ks, r, tile=None, split_first=False):
                if split_first:
                    split_lo(pool, *tile)
                first = 0 if table is u_rows else RANKS
                for k in ks:
                    wait(pool, row_used, ROWS * r + (k + 1 - ROWS))
                    pool.tensor_copy(expert_at[k % ROWS][:, :],
                                     expert[:, bass.ds(ROWS * r + (k - first), 1)]).then_inc(expert_at_ready, 1)
                pool.wait_ge(expert_at_ready, ROWS * r + (ks[-1] + 1))
                if not split_first:
                    split_lo(pool, *tile)
                for k in ks:
                    at = bass.IndirectOffsetOnAxis(ap=expert_at[k % ROWS][:, :], axis=0)
                    pool.indirect_dma_start(rows[:, k % ROWS, :], None, table, at).then_inc(gathered[k % ROWS], 16)

            pool.wait_ge(expert_ready, 1)
            for k in range(8):
                ks = [2 * k, 2 * k + 1] if k < AHEAD else [k + AHEAD]
                gather(u_rows, ks, 0, (S_U + 8 * O_IDLE + k, 0))
            with pool.Fori(1, R_PRE + R_MID) as r:
                for k in range(8):
                    gather(u_rows, [k + AHEAD], r, (S_U + 8 * O_IDLE + k, 2 * r))
            singles = 8 * (O_IDLE + R_PRE + R_MID)
            rank = ROWS * (R_PRE + R_MID) + AHEAD
            for k in range(singles, ETILES):
                n = 1 if k < singles + 2 else 3 if k in (118, 122) else 2
                assert rank >= RANKS or rank + n <= RANKS
                gather(u_rows if rank < RANKS else v_rows, range(rank, rank + n), 0, (S_U + k, 0), split_first=True)
                rank += n
            assert rank == RANKS + AHEAD
            with pool.Fori(0, OCTETS - 1) as o:
                for k in range(8):
                    gather(v_rows, [k + AHEAD + RANKS], o, (S_V + k, 2 * o))
            for k in range(8):
                tile = (N_TILES - 8 + k, 0)
                if k + AHEAD < 8:
                    gather(v_rows, [k + AHEAD + 2 * RANKS - 8], 0, tile)
                else:
                    split_lo(pool, *tile)
            for b in SHARED_Y:
                gain_and_bias(TB + b, ln2_gb)

        @block.scalar
        def _(act):
            for i in range(X_CHUNKS):
                act.wait_ge(xT_loaded[i], 16)
                act.activation(xT_hi[:, x_chunk(i), :], xT[:, x_chunk(i), :], ACT.Copy).then_inc(xT_hi_ready, 1)
            for c in range(S_LOOP):
                split_hi(act, c, 0)
            act.wait_ge(ff_loaded, 32)
            act.wait_ge(ff_ready, 1)
            act.activation(ff[0][:, :], banks[0:HEADS, 2, :], ACT.Identity, bias=ff_b[:, :]).then_inc(ff_step, 1)
            act.wait_ge(ff_step, 1)
            act.activation(ff[1][:, :], ff[0][:, :], ACT.Abs).then_inc(ff_step, 1)
            act.wait_ge(ff_step, 2)
            act.activation(ff[1][:, :], ff[1][:, :], ACT.Exp, scale=-1.0).then_inc(ff_step, 1)
            act.wait_ge(ff_step, 3)
            act.activation(ff[2][:, :], ff[1][:, :], ACT.Ln, bias=1.0).then_inc(ff_step, 1)

            def copy_proj(value, dst, bank, scale=1.0):
                act.wait_ge(tile_used, value)
                act.activation(dst, banks[:, bank, :], ACT.Copy, scale=scale).then_inc(proj_copied, 1)

            def copy_values(n, dst, bank):
                act.wait_ge(v_turned, n + 1)
                act.activation(dst[:, :, :].rearrange("p b d -> p (b d)"), banks[:, bank, :],
                               ACT.Copy).then_inc(proj_copied, 1)

            copy_proj(1, swa_k[:, :], 0)
            split_hi(act, S_LOOP, 0)
            copy_proj(2, vT[:, :], 1)
            split_hi(act, S_LOOP + 1, 0)
            PROJ_OUT = ((qT[:, :], HD ** -0.5), (kT[:, :], 1.0), (vT[:, :], 1.0),
                        (swa_q[:, :], HD ** -0.5))

            def projected(k, j):
                copy_proj(4 * j + (S_LOOP + k + 1), PROJ_OUT[k][0], k % 2, PROJ_OUT[k][1])
                if k < 3:
                    split_hi(act, S_LOOP + k + 2, j)

            copy_proj(3, qT[:, :], 0, HD ** -0.5)
            copy_values(0, swa_v, 1)
            split_hi(act, S_LOOP + 2, 0)
            act.wait_ge(small_loaded, 64)
            act.activation(ident_r[:, :], ident[:, :], ACT.Copy).then_inc(consts_ready, 1)
            act.activation(mask_r[:, :], cst[:, 0:P], ACT.Copy).then_inc(consts_ready, 1)
            projected(1, 0)
            act.activation(bias_r[:, :, :], cst[:, P:].rearrange("p (h k) -> p h k", h=HEADS),
                           ACT.Copy).then_inc(consts_ready, 1)
            projected(2, 0)
            projected(3, 0)
            copy_values(1, vv, 0)

            def outputs_hi(j, g):
                act.wait_ge(head_mixed, NU * j + SWA_UNITS * (g + 1))
                act.activation(mix_hi[:, bass.ds(j + PAIRS * g, 1), :].rearrange("p o t -> p (o t)"),
                               banks[:, 6 + g, :], ACT.Copy).then_inc(mix_hi_ready, 1)

            def pair(j, first=False, last=False):
                def exponentials(u):
                    kind, a, qb, k0, nk = UNITS[u]
                    act.wait_ge(max_ready, NU * j + (u + 1))
                    r = row[u % 3]
                    ins = act.activation(probs[u % 3][:, 0:nk * P], banks[:, 2 + u % 2, 0:nk * P], ACT.Exp,
                                         bias=r[:, 1:2], accum_out=r[:, 2:3])
                    if kind == "swa":
                        ins = act.activation(r[:, 3:4], sink[:, bass.ds(2 * j + a, 1)], ACT.Exp, bias=r[:, 1:2])
                    ins.then_inc(exp_ready, 1)

                def copy_turned(u):
                    kind, a, qb, k0, nk = UNITS[u]
                    act.wait_ge(turned, NU * j + (u + 1))
                    if u >= 2:
                        act.wait_ge(head_mixed, NU * j + (u - 1))
                    act.activation(probs_t[u % 2][:, 0:nk, :],
                                   banks[:, 4 + u % 2, 0:nk * P].rearrange("p (k q) -> p k q", k=nk),
                                   ACT.Copy).then_inc(turned_copied, 1)

                for step in range(STEPS + 1):
                    if step < NU:
                        exponentials(step)
                    if step == 1:
                        split_hi(act, S_LOOP + 5, j)
                    if step == OUTPUT_AT and not first:
                        outputs_hi(j - 1, 1)
                    if 0 <= step - TURN_LAG < NU:
                        copy_turned(step - TURN_LAG)
                    if step == SWA_UNITS + MIX_LAG:
                        outputs_hi(j, 0)
                    for begin, (k, n) in PROJ_AT.items():
                        if not last and step == begin + n:
                            projected(k, j + 1)
                if not last:
                    copy_values(j + 2, vv, 0)

            pair(0, first=True)
            with act.Fori(1, PAIRS - 1) as j:
                pair(j)
            pair(PAIRS - 1, last=True)
            outputs_hi(PAIRS - 1, 1)

            def square_root(b, n):
                act.wait_ge(ln_step, 3 * (n + 1))
                act.activation(rstd[:, b, 1:2], rstd[:, b, 0:1], ACT.Sqrt).then_inc(sqrt_ready, 1)

            def turned_hi(b):
                act.wait_ge(x1_turned, b + 1)
                act.activation(x1T_hi[:, :, bass.ts(b, P)],
                               banks[:, 2 * b:2 * b + 2, :].rearrange("p h (k t) -> p (h k) t", t=P),
                               ACT.Copy).then_inc(x1T_hi_ready, 1)

            def scale_rows(n):
                b, i = n % TB, shared_norm(n)
                act.wait_ge(factors_ready, i + 1)
                act.activation(x1[:, b, :], x1[:, b, :], ACT.Identity, bias=rstd[:, b, 5:6],
                               scale=rstd[:, b, 4:5]).then_inc(scaled, 1)

            for c in range(S_WOUT + 2, S_PQ + 2):
                split_hi(act, c, 0)
                for b in range(2):
                    if c == S_WOUT_B + 2 + b:
                        square_root(b, b)
                    if c == S_WOUT_B + TURN_AT + b + 1:
                        turned_hi(b)
                if c == S_PQ:
                    square_root(2, 2)
            scale_rows(2)
            square_root(3, 3)
            for b in range(2, TB):
                turned_hi(b)

            def copy_query(l, it):
                act.wait_ge(tile_used, 4 * it + (S_PQ + l + 1))
                wait(act, scored, 4 * it + (l - 1))
                act.activation(qh[l % 2][:, :], banks[:, l % 2, :], ACT.Copy).then_inc(qh_ready, 1)

            def copy_scores(l, it):
                act.wait_ge(scored, 4 * it + (l + 1))
                act.activation(scores[:, :, bass.ds(4 * it + l, 1), :].rearrange("p b o n -> p b (o n)"),
                               banks[:, 2 + l % 2, :].rearrange("p (b n) -> p b n", b=TB),
                               ACT.Copy).then_inc(scores_ready, 1)

            def query_group(it):
                for l in range(4):
                    copy_query(l, it)
                    split_hi(act, S_PQ + 2 + l, it)
                    if l or not isinstance(it, int):
                        copy_scores(l - 1, it)

            query_group(0)
            with act.Fori(1, LISTS // 4) as it:
                query_group(it)
            copy_scores(3, LISTS // 4 - 1)

            def gelu_tile(k, it, first=False, keep=None):
                act.wait_ge(tile_used, 4 * it + (S_U + k + 1))
                if keep is None and not first:
                    act.wait_ge(gelu_stored[k % 2], 32 * it + 16 * (k // 2))
                act.activation(gelu[k % 2][:, :] if keep is None else kept[:, keep, :], banks[:, k % 2, 0:DENSE], ACT.Gelu).then_inc(gelu_ready, 1)
                split_hi(act, S_U + 2 + k, it)

            for k in range(4):
                gelu_tile(k, 0, first=k < 2)
            with act.Fori(1, A_PRE // 4 - 1) as it:
                for k in range(4):
                    gelu_tile(k, it)

            for k in range(2):
                gelu_tile(k, A_PRE // 4 - 1)
            act.wait_ge(route_step, ROUTE_STEPS * TB)
            act.activation(sel[:, 2, :, :], sel[:, 2, :, :], ACT.Exp).then_inc(gate_exp, 1)
            gelu_tile(2, A_PRE // 4 - 1)
            for m in range(3):
                act.wait_ge(sel_turned, m + 1)
                act.activation(selT[:, m, :], banks[:, 2 + m, 0:DENSE], ACT.Copy).then_inc(selT_ready, 1)
            gelu_tile(3, A_PRE // 4 - 1)

            def stage_gates(chunk_half, o, tile, first):
                for g in range(2):
                    n = 2 * tile + g
                    act.wait_ge(scattered, 4 * TILES_PER_CHUNK * o + (2 * TILES_PER_CHUNK * chunk_half + n + 1))
                    if tile == 0 and g == 0 and not first:
                        act.wait_ge(g_stored[chunk_half], 16 * o)
                    t0 = tile * TOK_PER_TILE + 4 * g
                    act.activation(stage[chunk_half][:, :, t0:t0 + 4].rearrange("p n t -> p t n"),
                                   banks[:, 2 + g, :].rearrange("p (t n) -> p t n", t=4),
                                   ACT.Copy).then_inc(staged, 1)

            def two_chunks(o, first):
                for half in range(2):
                    for tile in range(TILES_PER_CHUNK):
                        gelu_tile(tile, 2 * o + (A_PRE // 4 + half))
                        stage_gates(half, o, tile, first)

            two_chunks(0, True)
            with act.Fori(1, O_MID) as o:
                two_chunks(o, False)
            def weight_hi(k, it, first=False):
                act.wait_ge(wgt_ready, 4 * it + (k + 1))
                if not first:
                    act.wait_ge(tile_used, 4 * it + (S_V + k - 1))
                act.activation(wgt_hi[k % 2][:, :], wgt[k % 2][:, :], ACT.Copy).then_inc(wgt_hi_ready, 1)

            for it in range((A_PRE + A_MID) // 4, ETILES // 4):
                if it == ETILES // 4 - 1:
                    weight_hi(0, 0, True)
                    weight_hi(1, 0, True)
                for k in range(4):
                    gelu_tile(k, it, keep=4 * it + k - A_PRE - A_MID)
            act.wait_ge(dots8_free, R_ALL + 1)
            act.activation(dots_gelu[:, :], dots[:, :], ACT.Gelu).then_inc(dots_gelu_ready, 1)

            with act.Fori(0, ETILES // 8 - 1) as i:
                for k in range(8):
                    split_hi(act, S_V + 2 + k, 2 * i)
                    weight_hi(2 + k, 2 * i)
            for k in range(6):
                split_hi(act, N_TILES - 6 + k, 0)
                weight_hi(ETILES - 6 + k, 0)
            for b in range(TB):
                square_root(b, TB + b)
                if b in SHARED_Y:
                    scale_rows(TB + b)

        @block.vector
        def _(dve):
            for i in range(X_CHUNKS):
                dve.wait_ge(xT_hi_ready, i + 1)
                dve.tensor_tensor(xT_lo[:, x_chunk(i), :], xT[:, x_chunk(i), :],
                                  xT_hi[:, x_chunk(i), :].bitcast(F32), ALU.subtract).then_inc(xT_lo_ready, 1)
            dve.wait_ge(small_loaded, 64)
            dve.tensor_scalar(neg_sink[:, :], sink[:, :], -1.0, None, ALU.mult).then_inc(consts_ready, 1)
            dve.memset(ff[3][:, :], 1.0).then_inc(max_step, 1)
            dve.wait_ge(ff_step, 4)
            dve.scalar_tensor_tensor(ff[1][:, :], ff[0][:, :], 0.0, ff[2][:, :], ALU.min, ALU.subtract).then_inc(ff_step, 1)
            dve.wait_ge(ff_step, 5)
            dve.wait_ge(max_step, 1)
            dve.tensor_tensor_scan(ff[2][:, :], ff[3][:, :], ff[1][:, :], 0.0, ALU.mult, ALU.add).then_inc(ff_step, 1)
            dve.wait_ge(ff_step, 6)
            dve.tensor_copy(decay_r[:, 0, :], ff[2][:, :]).then_inc(decay_ready, 1)
            dve.wait_ge(decay_ready, 3)
            dve.tensor_tensor(decay_r[:, 1, :], ff[2][:, :], decay_r[:, 0, :].bitcast(F32), ALU.subtract).then_inc(decay_ready, 1)
            dve.tensor_scalar(decay_r[:, 2, :], decay_r[:, 0, :].bitcast(F32), -1.0, None, ALU.mult).then_inc(decay_ready, 1)
            dve.wait_ge(decay_ready, 4)
            dve.tensor_scalar(decay_r[:, 3, :], decay_r[:, 1, :].bitcast(F32), -1.0, None, ALU.mult).then_inc(decay_ready, 1)

            def outputs_lo(j, g):
                dve.wait_ge(mix_hi_ready, 2 * j + (g + 1))
                s = bass.ds(j + PAIRS * g, 1)
                dve.tensor_tensor(mix_lo[:, s, :].rearrange("p o t -> p (o t)"), banks[:, 6 + g, :],
                                  mix_hi[:, s, :].rearrange("p o t -> p (o t)").bitcast(F32),
                                  ALU.subtract).then_inc(mix_lo_ready, 1)

            def pair(j, first=False):
                def maximum(u):
                    kind, a, qb, k0, nk = UNITS[u]
                    r = row[u % 3]
                    dve.wait_ge(logits_ready, NU * j + (u + 1))
                    src = banks[:, 2 + u % 2, 0:nk * P]
                    if kind == "fox":
                        dve.tensor_reduce(r[:, 1:2], src, AX_X, ALU.max, negate=True).then_inc(max_ready, 1)
                    else:
                        dve.tensor_reduce(r[:, 0:1], src, AX_X, ALU.max, negate=True).then_inc(max_step, 1)
                        dve.wait_ge(max_step, SWA_UNITS * j + (count_swa(u) + 2))
                        dve.tensor_tensor(r[:, 1:2], r[:, 0:1], neg_sink[:, bass.ds(2 * j + a, 1)],
                                          ALU.min).then_inc(max_ready, 1)

                def normalise(u):
                    kind, a, qb, k0, nk = UNITS[u]
                    r = row[u % 3]
                    dve.wait_ge(exp_ready, NU * j + (u + 1))
                    steps = (NU + SWA_UNITS) * j + (u + count_swa(u))
                    if kind == "fox":
                        dve.reciprocal(r[:, 4:5], r[:, 2:3]).then_inc(norm_step, 1)
                        dve.wait_ge(norm_step, steps + 1)
                    else:
                        dve.tensor_tensor(r[:, 5:6], r[:, 2:3], r[:, 3:4], ALU.add).then_inc(norm_step, 1)
                        dve.wait_ge(norm_step, steps + 1)
                        dve.reciprocal(r[:, 4:5], r[:, 5:6]).then_inc(norm_step, 1)
                        dve.wait_ge(norm_step, steps + 2)
                    dve.tensor_scalar(probs[u % 3][:, 0:nk * P], probs[u % 3][:, 0:nk * P], r[:, 4:5], None,
                                      ALU.mult).then_inc(probs_ready, 1)

                for step in range(STEPS):
                    if step < NU:
                        maximum(step)
                    if 1 <= step <= NU:
                        normalise(step - 1)
                    if step == OUTPUT_AT and not first:
                        outputs_lo(j - 1, 1)
                    if step == SWA_UNITS + MIX_LAG + 1:
                        outputs_lo(j, 0)

            pair(0, first=True)
            with dve.Fori(1, PAIRS) as j:
                pair(j)
            outputs_lo(PAIRS - 1, 1)

            ln_chain = [0]

            def chained(ins):
                ins.then_inc(norm_chain, 1)
                ln_chain[0] += 1
                dve.wait_ge(norm_chain, ln_chain[0])

            def add_residual(b, residual):
                chained(dve.scalar_tensor_tensor(x1[:, b, :], residual, ALPHA,
                                                 banks[:, 2 * b:2 * b + 2, :].rearrange("p h n -> p (h n)"),
                                                 ALU.mult, ALU.add))

            def begin_norm(b, n):
                for h in range(2):
                    ins = dve.bn_stats(stats[:, b, h, :], x1[:, b, bass.ts(h, 512)])
                ins.then_inc(ln_step, 1)
                dve.wait_ge(ln_step, 3 * n + 1)
                dve.bn_aggr(moments[:, b, :], stats[:, b, :, :]).then_inc(ln_step, 1)
                dve.wait_ge(ln_step, 3 * n + 2)
                dve.tensor_scalar(rstd[:, b, 0:1], moments[:, b, 1:2], EPS, None, ALU.add).then_inc(ln_step, 1)

            def finish_norm(b, n, gb=None, done=None):
                dve.wait_ge(sqrt_ready, n + 1)
                v, s, r0, t, r1 = (rstd[:, b, i:i + 1] for i in range(5))
                chained(dve.reciprocal(r0, s))
                chained(dve.scalar_tensor_tensor(t, r0, v, r0, ALU.mult, ALU.mult))
                chained(dve.tensor_scalar(t, t, -0.5, 1.5, ALU.mult, ALU.add))
                chained(dve.tensor_tensor(r1, r0, t, ALU.mult))
                if gb is None:
                    dve.scalar_tensor_tensor(rstd[:, b, 5:6], moments[:, b, 0:1], -1.0, r1,
                                             ALU.mult, ALU.mult).then_inc(factors_ready, 1)
                    return
                chained(dve.scalar_tensor_tensor(x1[:, b, :], x1[:, b, :], moments[:, b, 0:1], gb[:, 0, :],
                                                 ALU.subtract, ALU.mult))
                dve.scalar_tensor_tensor(x1[:, b, :], x1[:, b, :], r1, gb[:, 1, :],
                                         ALU.mult, ALU.add).then_inc(done, 1)

            dve.wait_ge(xR_loaded, 16)
            dve.wait_ge(ln_loaded, 16)

            def turned_lo(b):
                dve.wait_ge(x1T_hi_ready, b + 1)
                dve.tensor_tensor(x1T_lo[:, :, bass.ts(b, P)],
                                  banks[:, 2 * b:2 * b + 2, :].rearrange("p h (k t) -> p (h k) t", t=P),
                                  x1T_hi[:, :, bass.ts(b, P)].bitcast(F32), ALU.subtract).then_inc(x1T_lo_ready, 1)

            dve.wait_ge(tile_used, S_WOUT_B)
            for b in range(2):
                add_residual(b, xR[:, b, :])
                begin_norm(b, b)
            for b in range(2):
                finish_norm(b, b, ln1_gb, x1_ready)
            for b in range(2):
                turned_lo(b)
            dve.wait_ge(block_mixed, 1)
            add_residual(2, xR[:, 2, :])
            begin_norm(2, 2)
            dve.wait_ge(tile_used, S_PQ)
            add_residual(3, xR[:, 3, :])
            finish_norm(2, 2)
            begin_norm(3, 3)
            finish_norm(3, 3, ln1_gb, x1_ready)
            for b in range(2, TB):
                turned_lo(b)

            def dot(k, r):
                dve.wait_ge(gathered[k], 16 * r + 16)
                if k == 0:
                    dve.wait_ge(dots8_free, r + 1)
                dve.tensor_tensor_reduce(rows[:, k, :], rows[:, k, :], x1[:, 0, :], 1.0, 0.0, ALU.mult, ALU.add,
                                         dots8[:, k:k + 1]).then_inc(row_used, 1)

            def keep_dots(r):
                dve.wait_ge(row_used, ROWS * r + ROWS)
                dve.tensor_copy(dots[:, bass.ds(ROWS * r, ROWS)], dots8[:, :]).then_inc(dots8_free, 1)

            def route_block(b, between=None):
                n = [0]
                gap = [0]

                def other():
                    if between is not None:
                        between(gap[0])
                    gap[0] += 1

                def begin():
                    wait(dve, route_step, ROUTE_STEPS * b + n[0])
                    dve.sem_inc(route_tick, 1)

                def step(ins):
                    ins.then_inc(route_step, 1)
                    n[0] += 1

                def top16(vals, idx, src, count):
                    for l in range(count):
                        ins = dve.max(vals[:, l, 0:8], src[:, l, :])
                    step(ins)
                    other()
                    begin()
                    for l in range(count):
                        ins = dve.max_index(idx[:, l, 0:8], vals[:, l, 0:8], src[:, l, :])
                    step(ins)
                    other()
                    begin()
                    for l in range(count):
                        ins = dve.match_replace(src[:, l, :], vals[:, l, 0:8], src[:, l, :], NEG_MAX)
                    step(ins)
                    other()
                    begin()
                    for l in range(count):
                        ins = dve.max(vals[:, l, 8:16], src[:, l, :])
                    step(ins)
                    other()
                    begin()
                    for l in range(count):
                        ins = dve.max_index(idx[:, l, 8:16], vals[:, l, 8:16], src[:, l, :])
                    step(ins)
                    other()
                    begin()

                begin()
                step(dve.tensor_copy(work[:, :, :], scores[:, bass.ds(b, 1), :, :].rearrange("p o l n -> p (o l) n")))
                begin()
                top16(best, best_i, work, LISTS)
                step(dve.tensor_copy(best_f[:, :, :], best_i[:, :, :]))
                halves = best[:, :, :].rearrange("p (h s) k -> p h s k", s=2)
                step(dve.tensor_tensor(cand[:, :, :].rearrange("p h (i j) -> p h i j", j=TOPK),
                                       halves[:, :, 0, :].unsqueeze(3).to_broadcast([P, PH, TOPK, TOPK]),
                                       halves[:, :, 1, :].unsqueeze(2).to_broadcast([P, PH, TOPK, TOPK]), ALU.add))
                begin()
                top16(top, top_i, cand, PH)
                flat_i = top_i[:, :, :].rearrange("p h k -> p (h k)")
                step(dve.tensor_scalar(pos_u[:, 0, :], flat_i, 4, None, ALU.logical_shift_right))
                step(dve.tensor_scalar(pos_u[:, 1, :], flat_i, TOPK - 1, None, ALU.bitwise_and))
                begin()
                step(dve.tensor_copy(pos_f[:, :, :], pos_u[:, :, :]))
                step(dve.tensor_tensor(sel[:, 2, bass.ds(b, 1), :].rearrange("p o (h k) -> p (o h) k", k=TOPK), top[:, :, :],
                                       top[:, :, 0:1].to_broadcast([P, PH, TOPK]), ALU.subtract))
                begin()
                ids = best_f[:, :, :].rearrange("p (h s) k -> p h s k", s=2)
                for s in range(2):
                    step(dve.tensor_tensor(match[:, :, :].rearrange("p h (k j) -> p (h k) j", j=TOPK),
                                           pos_f[:, s, :].unsqueeze(2).to_broadcast([P, P, TOPK]),
                                           iota[:, 0:TOPK].unsqueeze(1).to_broadcast([P, P, TOPK]), ALU.is_equal))
                    other()
                    begin()
                    step(dve.tensor_tensor(prod[:, :, :].rearrange("p (h a) (k j) -> p h (a k) j", a=2, j=TOPK),
                                           match[:, :, :].rearrange("p h (k j) -> p h k j", j=TOPK),
                                           ids[:, :, s, :].unsqueeze(2).to_broadcast([P, PH, TOPK, TOPK]), ALU.mult))
                    other()
                    begin()
                    ins = dve.tensor_reduce(sel[:, s, bass.ds(b, 1), :].rearrange("p o n -> p (o n)"),
                                            prod[:, :, :].rearrange("p l (k j) -> p (l k) j", j=TOPK), AX_X, ALU.add)
                    step(ins)
                    other()
                    begin()
                ROUTE_SEEN[0] = n[0]

            ROUTE_SEEN = [0]
            dve.wait_ge(scores_ready, LISTS)
            route_block(0)
            dve.wait_ge(route_step, ROUTE_STEPS)
            dve.memset(dots8[:, :], 0.0).then_inc(dots8_free, 1)
            dve.scalar_tensor_tensor(expert[:, :], sel[:, 0, 0, :], float(NKEY), sel[:, 1, 0, :],
                                     ALU.mult, ALU.add).then_inc(expert_ready, 1)
            with dve.Fori(1, TB) as b:
                done = [0]

                def some_dots(i):
                    for _ in range(2 if i < 5 else int(i in (5, 7, 9, 10, 12, 14))):
                        n = done[0]
                        done[0] += 1
                        dot(n % ROWS, 2 * b + (n // ROWS - 2))
                        if n % ROWS == ROWS - 1:
                            keep_dots(2 * b + (n // ROWS - 2))
                route_block(b, some_dots)
                assert done[0] == 2 * ROWS
            assert ROUTE_SEEN[0] == ROUTE_STEPS, ROUTE_SEEN

            gates = sel[:, 2, :, :].rearrange("p b (h k) -> p (b h) k", k=TOPK)
            dve.wait_ge(gate_exp, 1)
            dve.tensor_reduce(gsum[:, 0, :], gates, AX_X, ALU.add).then_inc(gate_step, 1)
            dve.wait_ge(gate_step, 1)
            dve.reciprocal(gsum[:, 1, :], gsum[:, 0, :]).then_inc(gate_step, 1)
            dve.wait_ge(gate_step, 2)
            dve.tensor_tensor(gates, gates, gsum[:, 1, :].unsqueeze(2).to_broadcast([P, TB * PH, TOPK]),
                              ALU.mult).then_inc(gates_ready, 1)
            for k in range(H_DOT):
                dot(k, R_PRE)
            dve.wait_ge(selT_ready, 3)
            dve.tensor_copy(gate_r[:, :], selT[:, 2, :]).then_inc(gate_step, 1)
            dve.wait_ge(gate_step, 3)
            dve.tensor_copy(gateT_hi[:, :], gate_r[:, :].bitcast(F32)).then_inc(gate_step, 1)
            dve.tensor_tensor(gateT_lo[:, :], selT[:, 2, :], gate_r[:, :].bitcast(F32), ALU.subtract).then_inc(gate_step, 1)
            dve.wait_ge(gate_step, 5)

            def one_hots(tile, o, first):
                slot = tile % 2
                if not first:
                    dve.wait_ge(scattered, 16 * o + (2 * tile - 2))
                if tile or not isinstance(o, int):
                    dve.wait_ge(onehot_ready, 8 * o + tile)
                t = bass.ds(2 * CHUNK * o + TOK_PER_TILE * tile, TOK_PER_TILE)
                shape = [P, TOK_PER_TILE, NKEY]
                row_of = iota[:, :].unsqueeze(1).to_broadcast(shape)

                def col(ap):
                    return ap.unsqueeze(2).to_broadcast(shape)

                dve.tensor_tensor(is_i1[:, :, :], row_of, col(selT[:, 0, t]), ALU.is_equal).then_inc(is_i1_ready, 1)
                dve.tensor_tensor(onehot[slot][0][:, :, :], row_of, col(selT[:, 1, t]), ALU.is_equal)
                dve.wait_ge(is_i1_ready, 8 * o + (tile + 1))
                dve.tensor_tensor(onehot[slot][1][:, :, :], is_i1[:, :, :], col(gateT_hi[:, t]), ALU.mult)
                dve.tensor_tensor(onehot[slot][2][:, :, :], is_i1[:, :, :], col(gateT_lo[:, t]),
                                  ALU.mult).then_inc(onehot_ready, 1)

            def two_chunks(o, first):
                for tile in range(8):
                    one_hots(tile, o, first and tile < 2)
                    dot((tile + H_DOT) % ROWS, o + (R_PRE + (tile + H_DOT) // ROWS))
                    if tile + H_DOT == ROWS - 1:
                        keep_dots(o + R_PRE)

            two_chunks(0, True)
            with dve.Fori(1, O_MID) as o:
                two_chunks(o, False)
            def weights(k, i):
                it, group = 2 * i, k // 4
                fewer = (KEPT + 1 - group) // 2
                is_kept = isinstance(i, int) and 8 * i + k < A_POST
                if k % 4 == 0:
                    dve.wait_ge(comb_loaded[group], 16 * (i + 1) if is_kept else 32 * i + (32 - 16 * fewer))
                if not isinstance(i, int) or i or k >= 2:
                    dve.wait_ge(wgt_lo_ready, 4 * it + (k - 1))
                dve.tensor_tensor(wgt[k % 2][:, :].rearrange("p (c t) -> p c t", c=CHUNKS),
                                  (kept[:, 8 * i + k, :] if is_kept else ga[group][:, k % 4, :]
                                   ).rearrange("p (c t) -> p c t", c=CHUNKS),
                                  gg[group][:, :, k % 4, :], ALU.mult).then_inc(wgt_ready, 1)

            def weight_lo(k, it):
                dve.wait_ge(wgt_hi_ready, 4 * it + (k + 1))
                dve.tensor_tensor(wgt_lo[k % 2][:, :], wgt[k % 2][:, :], wgt_hi[k % 2][:, :].bitcast(F32),
                                  ALU.subtract).then_inc(wgt_lo_ready, 1)

            for r in range(R_PRE + R_MID, R_ALL):
                if r == R_ALL - 1:
                    dve.wait_ge(g_stored[0], 16 * CHUNKS // 2)
                    dve.wait_ge(g_stored[1], 16 * CHUNKS // 2)
                    dve.wait_ge(gelu_ready, A_PRE + A_MID + 2)
                    for k in range(2):
                        weights(k, 0)
                    for k in range(2):
                        weight_lo(k, 0)
                for k in range(H_DOT if r == R_PRE + R_MID else 0, ROWS):
                    dot(k, r)
                keep_dots(r)
            dve.wait_ge(dots_gelu_ready, 1)
            dve.tensor_tensor(row_weight[:, :], dots_gelu[:, :], sel[:, 2, 0, :], ALU.mult).then_inc(row_weight_ready, 1)
            dve.tensor_scalar(x1[:, 0, :], x1[:, 0, :], ALPHA, None, ALU.mult).then_inc(residual_ready, 1)
            dve.wait_ge(row_weight_ready, 1)

            def add_row(k, r):
                dve.wait_ge(gathered[k], 16 * r + 16 * (R_ALL + 1))
                dve.wait_ge(row_used, ROWS * r + (RANKS + k))
                dve.scalar_tensor_tensor(x1[:, 0, :], rows[:, k, :], row_weight[:, bass.ds(ROWS * r + k, 1)],
                                         x1[:, 0, :], ALU.mult, ALU.add).then_inc(row_used, 1)

            dve.wait_ge(gelu_ready, ETILES)
            dve.wait_ge(residual_ready, 1)

            def octet(i, made=0):
                for k in range(8):
                    if k >= made:
                        weights(k, i)
                    add_row(k, i)
                    if k >= made:
                        weight_lo(k, 2 * i)

            octet(0, made=2)
            octet(1)
            with dve.Fori(2, OCTETS) as i:
                octet(i)

            dve.wait_ge(ln_loaded, 32)
            dve.wait_ge(row_used, 2 * RANKS)
            begin_norm(0, TB)
            finish_norm(0, TB)
            for b in range(1, TB):
                dve.wait_ge(combined, b)
                add_residual(b, x1[:, b, :])
                if b > 1:
                    finish_norm(b - 1, TB + b - 1)
                begin_norm(b, TB + b)
            finish_norm(TB - 1, 2 * TB - 1, ln2_gb, y_ready)

        @block.tensor
        def _(pe):
            pe.wait_ge(ff_loaded, 16)
            for k in range(KT):
                if k % (KT // X_CHUNKS) == 0:
                    pe.wait_ge(xT_loaded[k * X_CHUNKS // KT], 16)
                ins = pe.matmul(banks[0:HEADS, 2, :], ff_w[:, k, :], xT[:, k, :], start=(k == 0), stop=(k == KT - 1))
            ins.then_inc(ff_ready, 1)
            pe.wait_ge(xT_lo_ready, X_CHUNKS)

            def features(c, it, bank, hiT, loT, part=0, parts=1, tokens=slice(0, SEQ), at=0, last=True):
                if part == 0:
                    pe.wait_ge(lo_ready, 4 * it + (c + 1))
                h, l = hi[c % PART_SLOTS], lo[c % PART_SLOTS]
                o = banks[:, bank, at:at + tokens.stop - tokens.start]
                for k in range(part * KT // parts, (part + 1) * KT // parts):
                    s = bass.ts(k, P)
                    pe.matmul(o, h[:, s], hiT[:, k, tokens], start=(k == 0), stop=False)
                    pe.matmul(o, h[:, s], loT[:, k, tokens], start=False, stop=False)
                    ins = pe.matmul(o, l[:, s], hiT[:, k, tokens], start=False, stop=(k == KT - 1))
                if last and part == parts - 1:
                    ins.then_inc(tile_used, 1)

            def turn_values(copied, bank):
                pe.wait_ge(proj_copied, copied)
                for b in range(TB):
                    ins = pe.transpose(banks[:, bank, bass.ts(b, P)], vT[:, bass.ts(b, P)], ident[:, :])
                ins.then_inc(v_turned, 1)

            def project(k, j, part=0, parts=1, copied=None):
                if part == 0:
                    pe.wait_ge(proj_copied, pair_copies(j) + max(k - 1, 0) if copied is None else copied)
                features(S_LOOP + k, j, k % 2, xT_hi, xT_lo, part, parts)

            features(0, 0, 0, xT_hi, xT_lo)
            features(1, 0, 1, xT_hi, xT_lo)
            project(0, 0, copied=1)
            pe.wait_ge(small_loaded, 64)
            turn_values(2, 1)
            project(1, 0, copied=4)
            project(2, 0, copied=4)
            project(3, 0)
            turn_values(pair_copies(0) + 3, 0)
            pe.wait_ge(consts_ready, 4)

            def combine_block(b, c, parts, start, stop):
                h, l = hi[c % PART_SLOTS], lo[c % PART_SLOTS]
                h_at, l_at = parts
                for n in range(2):
                    o, s = banks[:, 2 * b + n, :], bass.ts(n, 512)
                    pe.matmul(o, h_at(b), h[:, s], start=start, stop=False)
                    pe.matmul(o, h_at(b), l[:, s], start=False, stop=False)
                    ins = pe.matmul(o, l_at(b), h[:, s], start=False, stop=stop)
                return ins

            def mixed(r):
                return (lambda b: mix_hi[:, r, bass.ts(b, P)], lambda b: mix_lo[:, r, bass.ts(b, P)])

            def pair(j, first=False, last=False):
                def logits(u):
                    kind, a, qb, k0, nk = UNITS[u]
                    hs = slice(a * HD, (a + 1) * HD)
                    qs = bass.ts(qb, P)
                    o = banks[:, 2 + u % 2, 0:nk * P]
                    if u >= 2:
                        pe.wait_ge(exp_ready, NU * j + (u - 1))
                    if u == 0:
                        pe.wait_ge(proj_copied, pair_copies(j) + 2)
                        pe.wait_ge(decay_loaded, 32 * j + 32)
                    if u == SWA_UNITS:
                        pe.wait_ge(proj_copied, pair_copies(j) + 4)
                    if kind == "fox":
                        pe.matmul(o, qT[hs, qs], kT[hs, 0:nk * P], start=True, stop=False)
                        pe.matmul(o[:, (nk - 1) * P:], ident_r[:, :], mask_r[:, :], start=False, stop=False)
                        pe.matmul(o, decay_q[:, a, qs], decay_k[:, a, 0:nk * P], start=False, stop=True).then_inc(logits_ready, 1)
                    else:
                        pe.matmul(o, swa_q[hs, qs], swa_k[hs, k0 * P:(k0 + nk) * P], start=True, stop=False)
                        pe.matmul(o, ident_r[:, :],
                                  bias_r[:, bass.ds(2 * j + a, 1), (2 - nk) * P:].rearrange("p o k -> p (o k)"),
                                  start=False, stop=True).then_inc(logits_ready, 1)

                def turn(u):
                    kind, a, qb, k0, nk = UNITS[u]
                    pe.wait_ge(probs_ready, NU * j + (u + 1))
                    if u >= 2:
                        pe.wait_ge(turned_copied, NU * j + (u - 1))
                    for k in range(nk):
                        ins = pe.transpose(banks[:, 4 + u % 2, bass.ts(k, P)], probs[u % 3][:, bass.ts(k, P)], ident[:, :])
                    ins.then_inc(turned, 1)

                def mix(u):
                    kind, a, qb, k0, nk = UNITS[u]
                    hs = slice(a * HD, (a + 1) * HD)
                    pe.wait_ge(turned_copied, NU * j + (u + 1))
                    if u == 0:
                        pe.wait_ge(proj_copied, pair_copies(j) + 5)
                    if u in (0, SWA_UNITS) and not first:
                        pe.wait_ge(mix_lo_ready, 2 * j - (u == 0))
                    o = banks[hs, 6 + (kind == "swa"), bass.ts(qb, P)]
                    val = vv if kind == "fox" else swa_v
                    for k in range(nk):
                        ins = pe.matmul(o, val[:, k0 + k, hs], probs_t[u % 2][:, k, :], start=(k == 0), stop=(k == nk - 1))
                    ins.then_inc(head_mixed, 1)

                for step in range(STEPS):
                    if step < NU:
                        logits(step)
                    if 0 <= step - TURN_LAG < NU:
                        turn(step - TURN_LAG)
                    if 0 <= step - MIX_LAG:
                        mix(step - MIX_LAG)
                    for begin, (k, n) in PROJ_AT.items():
                        if not last and begin <= step < begin + n:
                            project(k, j + 1, step - begin, n)
                if not last:
                    turn_values(pair_copies(j + 1) + 3, 0)

            pair(0, first=True)
            with pe.Fori(1, PAIRS - 1) as j:
                pair(j)
            pair(PAIRS - 1, last=True)

            def combine(c, parts, blocks, start):
                for b in blocks:
                    ins = combine_block(b, c, parts, start, False)
                ins.then_inc(tile_used, 1)

            def turn_x1(b):
                if b in SHARED_X:
                    pe.wait_ge(shared_done, shared_norm(b) + 1)
                else:
                    pe.wait_ge(x1_ready, b + 1 - (b > 2))
                for k in range(KT):
                    ins = pe.transpose(banks[:, 2 * b + k // 4, bass.ts(k % 4, P)], x1[:, b, bass.ts(k, P)], ident[:, :])
                ins.then_inc(x1_turned, 1)

            for r in range(KT):
                pe.wait_ge(mix_lo_ready, 2 * PAIRS - (r < KT - 1))
                pe.wait_ge(lo_ready, S_WOUT + r + 1)
                for b in range(2):
                    ins = combine_block(b, S_WOUT + r, mixed(r), r == 0, r == KT - 1)
                ins.then_inc(tile_used, 1)
            for r in range(KT - 2):
                if r >= TURN_AT:
                    turn_x1(r - TURN_AT)
                pe.wait_ge(lo_ready, S_WOUT_B + r + 1)
                combine(S_WOUT_B + r, mixed(r), range(2, TB), r == 0)
            turn_x1(KT - 2 - TURN_AT)
            pe.wait_ge(lo_ready, S_PQ - 1)
            combine(S_PQ - 2, mixed(KT - 2), range(2, TB), False)
            pe.wait_ge(lo_ready, S_PQ)
            combine_block(2, S_PQ - 1, mixed(KT - 1), False, True).then_inc(block_mixed, 1)
            combine_block(3, S_PQ - 1, mixed(KT - 1), False, True).then_inc(tile_used, 1)

            def query_half(l, half):
                features(S_PQ + l, 0, l, x1T_hi, x1T_lo, tokens=slice(2 * P * half, 2 * P * (half + 1)),
                         at=2 * P * half, last=half == 1)

            pe.wait_ge(x1T_lo_ready, 2)
            for l in range(2):
                query_half(l, 0)
            for b in range(2, TB):
                turn_x1(b)
            pe.wait_ge(x1T_lo_ready, TB)

            def score(l, it):
                if isinstance(it, int) and it == 0 and l == 0:
                    pe.wait_ge(keys_loaded, 16)
                pe.wait_ge(qh_ready, 4 * it + (l + 1))
                wait(pe, scores_ready, 4 * it + (l - 1))
                for b in range(TB):
                    ins = pe.matmul(banks[:, 2 + l % 2, bass.ts(b, P)], qh[l % 2][:, bass.ts(b, P)],
                                    keys[:, bass.ds(4 * it + l, 1), :].rearrange("p o n -> p (o n)"),
                                    start=True, stop=True)
                ins.then_inc(scored, 1)

            def query_group(it):
                for l in range(4):
                    wait(pe, qh_ready, 4 * it + (l - 1))
                    if isinstance(it, int) and l < 2:
                        query_half(l, 1)
                    else:
                        features(S_PQ + l, it, l % 2, x1T_hi, x1T_lo)
                    if l or not isinstance(it, int):
                        score(l - 1, it)

            query_group(0)
            with pe.Fori(1, LISTS // 4) as it:
                query_group(it)
            score(3, LISTS // 4 - 1)

            def expert_tile(k, it, first=False):
                if first:
                    pe.wait_ge(qh_ready, LISTS)
                else:
                    pe.wait_ge(gelu_ready, 4 * it + (k - 1))
                features(S_U + k, it, k % 2, x1T_hi, x1T_lo, tokens=slice(P, SEQ))

            for k in range(4):
                expert_tile(k, 0, first=k < 2)
            with pe.Fori(1, A_PRE // 4 - 1) as it:
                for k in range(4):
                    expert_tile(k, it)
            for k in range(3):
                expert_tile(k, A_PRE // 4 - 1)
            pe.wait_ge(gates_ready, 1)
            for m in range(3):
                for b in range(1, TB):
                    ins = pe.transpose(banks[:, 2 + m, bass.ts(b - 1, P)], sel[:, m, b, :], ident[:, :])
                ins.then_inc(sel_turned, 1)
            expert_tile(3, A_PRE // 4 - 1)
            pe.wait_ge(selT_ready, 3)

            def scatter(tile, o, first):
                slot = tile % 2
                pe.wait_ge(onehot_ready, 8 * o + (tile + 1))
                for g in range(2):
                    if not first:
                        pe.wait_ge(staged, 16 * o + (2 * tile + g - 1))
                    for k in range(4 * g, 4 * g + 4):
                        r = banks[:, 2 + g, bass.ts(k % 4, NKEY)]
                        pe.matmul(r, onehot[slot][0][:, k, :], onehot[slot][1][:, k, :], start=True, stop=False)
                        ins = pe.matmul(r, onehot[slot][0][:, k, :], onehot[slot][2][:, k, :], start=False, stop=True)
                    ins.then_inc(scattered, 1)

            def two_chunks(o, first):
                for tile in range(8):
                    expert_tile(tile % 4, 2 * o + (A_PRE // 4 + tile // 4))
                    scatter(tile, o, first and tile == 0)

            two_chunks(0, True)
            with pe.Fori(1, O_MID) as o:
                two_chunks(o, False)
            for it in range((A_PRE + A_MID) // 4, ETILES // 4):
                for k in range(4):
                    expert_tile(k, it)

            pe.wait_ge(staged, DENSE // 4)

            def experts(k, it, start=False, last=False):
                pe.wait_ge(lo_ready, 4 * it + (S_V + k + 1))
                pe.wait_ge(wgt_lo_ready, 4 * it + (k + 1))
                if last:
                    for b in range(1, TB):
                        combine_block(b, S_V + k, weighted(k), False, True).then_inc(combined, 1)
                else:
                    combine(S_V + k, weighted(k), range(1, TB), start)

            def weighted(k):
                return (lambda b: wgt_hi[k % 2][:, bass.ts(b - 1, P)], lambda b: wgt_lo[k % 2][:, bass.ts(b - 1, P)])

            for k in range(8):
                experts(k, 0, start=k == 0)
            with pe.Fori(1, ETILES // 8 - 1) as i:
                for k in range(8):
                    experts(k, 2 * i)
            for k in range(ETILES - 8, ETILES):
                experts(k, 0, last=k == ETILES - 1)


def kernel(x, ln1_g, ln1_b, w_in, b_f, sink, w_out, ln2_g, ln2_b, w_pq, peer_keys1, peer_keys2, peer_u, peer_v):
    import numpy as np
    import concourse.bacc as bacc
    from concourse.bass_utils import run_bass_kernel_spmd

    def tiles(w):
        n = w.shape[1] // P
        return np.ascontiguousarray(w.reshape(KT, P, n, P).transpose(2, 1, 0, 3)).reshape(n, P, D)

    x, w_in, w_out = np.asarray(x)[0], np.asarray(w_in)[0], np.asarray(w_out)[0]
    fox_q, fox_k, fox_v, w_f, swa_q, swa_k, swa_v = np.split(w_in, [512, 1024, 1536, 1544, 2056, 2184], axis=1)
    order = [h for j in range(PAIRS) for h in (j, PAIRS + j)]
    swa_q = swa_q.reshape(D, HEADS, HD)[:, order].reshape(D, HEADS * HD)
    swa_rows = w_out[512:].reshape(HEADS, HD, D)[order].reshape(HEADS * HD, D)
    fq, fk, fv, sq = tiles(fox_q), tiles(fox_k), tiles(fox_v), tiles(swa_q)
    looped = [t[j] for j in range(PAIRS) for t in (fq, fk, fv, sq)]
    w1 = np.stack([tiles(swa_k)[0], tiles(swa_v)[0], *looped, *w_out[:512].reshape(4, P, D), *swa_rows.reshape(4, P, D)])

    blocked = -2.0 ** 100
    i = np.arange(P)
    mask = np.where(i[None, :] <= i[:, None], 0.0, blocked)
    key = np.arange(SWA_KEYS)[None, :] - P
    chunks_back = i[:, None] // 64 - key // 64
    seen = (chunks_back >= 0) & (chunks_back <= 1)
    slopes = 2.0 ** -(np.array(order) + 1.0)
    bias = np.where(seen[:, None, :], -slopes[None, :, None] * np.abs(i[:, None] - key)[:, None, :], blocked)
    consts = np.concatenate([mask, bias.reshape(P, -1), np.eye(P), np.tile(i, (P, 1))], axis=1).astype(np.float32)

    keys = np.stack([np.asarray(peer_keys1)[0], np.asarray(peer_keys2)[0]], axis=1).reshape(LISTS, NKEY, P)
    u = np.asarray(peer_u)[0]
    arrays = {
        "x_t": x.T.reshape(KT, P, SEQ).transpose(1, 0, 2),
        "x_rows": x.reshape(TB, P, D).transpose(1, 0, 2),
        "w1": w1,
        "w_ff": w_f.reshape(KT, P, HEADS).transpose(1, 0, 2),
        "b_f": np.asarray(b_f).reshape(HEADS, 1),
        "sinks": np.broadcast_to(np.asarray(sink)[0][order], (P, HEADS)),
        "ln_par": np.broadcast_to(np.stack([np.asarray(a)[0] for a in (ln1_g, ln1_b, ln2_g, ln2_b)]), (P, 4, D)),
        "w_pq": tiles(np.asarray(w_pq)[0]),
        "keys_t": keys.transpose(2, 0, 1),
        "u_t": u.reshape(ETILES, P, KT, P).transpose(0, 3, 2, 1).reshape(ETILES, P, D),
        "u_rows": u,
        "v_tab": np.asarray(peer_v)[0].reshape(ETILES, P, D),
        "consts": consts,
    }
    arrays = {n: np.ascontiguousarray(a) for n, a in arrays.items()}
    nc = bacc.Bacc("TRN2", target_bir_lowering=False, num_devices=1)
    args = [nc.dram_tensor(n, a.shape, F32, kind="ExternalInput").ap() for n, a in arrays.items()]
    args.append(nc.dram_tensor("out", (SEQ, D), F32, kind="ExternalOutput").ap())
    build(nc, *args)
    r = run_bass_kernel_spmd(nc, [arrays], core_ids=[0])
    return r.results[0]["out"].reshape(1, SEQ, D)
```
